# Optimizing a Trainium2 kernel written in Bass

```python
import math
import jax, jax.numpy as jnp
from jax import lax
import numpy as np

D_MODEL = 1024
BATCH = 1
SEQ = 256
DEPTH = 1

RET_HEADS = 4
RET_QK_DIM = 128
RET_V_DIM = 256
RET_CHUNK = 128
RET_QK_W = RET_HEADS * RET_QK_DIM
RET_V_W = RET_HEADS * RET_V_DIM
NA_HEADS = 8
NA_HEAD_DIM = 64
NA_W = NA_HEADS * NA_HEAD_DIM
GRID_W = 64
NA_WIN_ROWS = 8
NA_WIN_COLS = 16
NA_Q_BLOCK_COLS = 16
NA_K_BLOCK_COLS = 32
NA_REL_ROWS = 2 * NA_WIN_ROWS - 1
NA_REL_COLS = 2 * NA_WIN_COLS - 1
D_FF = 2816
RMS_EPS = 1e-6
ROPE_BASE = 10000.0
NEG_INF = -1e30
MIX_SPLITS = (RET_QK_W, RET_QK_W, RET_V_W, RET_V_W, NA_W, NA_W, NA_W, D_MODEL, D_MODEL)
MIX_IN_W = sum(MIX_SPLITS)


def _rms_norm(x, gain):
    xf = x.astype(jnp.float32)
    y = xf * lax.rsqrt(jnp.mean(xf * xf, axis=-1, keepdims=True) + RMS_EPS)
    return (y * gain.astype(jnp.float32)).astype(x.dtype)

def _swiglu(x, w_in, w_out):
    g, u = jnp.split(x @ w_in, 2, axis=-1)
    return (jax.nn.silu(g) * u) @ w_out

def _rotary(x, pos):
    half = x.shape[-1] // 2
    inv = 1.0 / (ROPE_BASE ** jnp.linspace(0.0, 1.0, half, dtype=jnp.float32))
    ang = pos[:, None] * inv[None, :]
    cos, sin = jnp.cos(ang), jnp.sin(ang)
    x1, x2 = x[..., :half], x[..., half:]
    return jnp.concatenate([x1 * cos - x2 * sin, x1 * sin + x2 * cos], axis=-1)

def _retention_one_dir(q, k, v, log_gamma, strict):
    B, H, S, DK = q.shape
    DV = v.shape[-1]
    C = RET_CHUNK
    N = S // C
    qc = q.reshape(B, H, N, C, DK)
    kc = k.reshape(B, H, N, C, DK)
    vc = v.reshape(B, H, N, C, DV)
    idx = jnp.arange(C, dtype=jnp.float32)
    diff = idx[:, None] - idx[None, :]
    lower = (diff > 0) if strict else (diff >= 0)
    intra = jnp.where(lower[None], jnp.exp(log_gamma[:, None, None] * jnp.where(lower, diff, 0.0)[None]), 0.0)
    scores = jnp.einsum('bhnqd,bhnkd->bhnqk', qc, kc) * intra[None, :, None]
    inner = jnp.einsum('bhnqk,bhnkv->bhnqv', scores, vc)
    k_dec = jnp.exp(log_gamma[:, None] * (C - 1 - idx)[None, :])
    upd = jnp.einsum('bhnkd,bhnkv->nbhdv', kc * k_dec[None, :, None, :, None], vc)
    chunk_dec = jnp.exp(log_gamma * C)[None, :, None, None]

    def step(state, u):
        return chunk_dec * state + u, state

    _, prev = lax.scan(step, jnp.zeros((B, H, DK, DV), jnp.float32), upd)
    q_dec = jnp.exp(log_gamma[:, None] * (idx + 1.0)[None, :])
    cross = jnp.einsum('bhnqd,nbhdv->bhnqv', qc * q_dec[None, :, None, :, None], prev)
    return (inner + cross).reshape(B, H, S, DV)

def _bidirectional_retention(q, k, v, decay_fwd_logit, decay_bwd_logit):
    lg_f = jax.nn.log_sigmoid(decay_fwd_logit.astype(jnp.float32))
    lg_b = jax.nn.log_sigmoid(decay_bwd_logit.astype(jnp.float32))
    y_f = _retention_one_dir(q, k, v, lg_f, strict=False)
    flip = lambda a: jnp.flip(a, axis=2)
    y_b = flip(_retention_one_dir(flip(q), flip(k), flip(v), lg_b, strict=True))
    return y_f + y_b

def _neighborhood_attention(q, k, v, rel_bias):
    B, S, NH, DH = q.shape
    rows = S // GRID_W
    kr = min(NA_WIN_ROWS, rows)
    ncb = GRID_W // NA_Q_BLOCK_COLS
    qg = (q * (DH ** -0.5)).reshape(B, rows, GRID_W, NH, DH)
    kg = k.reshape(B, rows, GRID_W, NH, DH)
    vg = v.reshape(B, rows, GRID_W, NH, DH)
    c0 = jnp.arange(ncb, dtype=jnp.int32) * NA_Q_BLOCK_COLS
    q_cols = c0[:, None] + jnp.arange(NA_Q_BLOCK_COLS, dtype=jnp.int32)[None, :]
    key_cols = (jnp.clip(c0 - NA_WIN_COLS // 2, 0, GRID_W - NA_K_BLOCK_COLS)[:, None]
                + jnp.arange(NA_K_BLOCK_COLS, dtype=jnp.int32)[None, :])
    win_start = jnp.clip(q_cols - NA_WIN_COLS // 2, 0, GRID_W - NA_WIN_COLS)
    kcb = key_cols[:, None, :]
    col_mask = (kcb >= win_start[:, :, None]) & (kcb < win_start[:, :, None] + NA_WIN_COLS)
    col_idx = jnp.clip(kcb - q_cols[:, :, None] + NA_WIN_COLS - 1, 0, NA_REL_COLS - 1)

    def row_block(r):
        rs = jnp.clip(r - kr // 2, 0, rows - kr)
        q_r = lax.dynamic_index_in_dim(qg, r, axis=1, keepdims=False).reshape(B, ncb, NA_Q_BLOCK_COLS, NH, DH)
        k_blk = lax.dynamic_slice_in_dim(kg, rs, kr, axis=1)[:, :, key_cols]
        v_blk = lax.dynamic_slice_in_dim(vg, rs, kr, axis=1)[:, :, key_cols]
        s = jnp.einsum('bnqhd,brnkhd->bhnqrk', q_r, k_blk).astype(jnp.float32)
        row_idx = rs + jnp.arange(kr, dtype=jnp.int32) - r + NA_WIN_ROWS - 1
        bias = rel_bias[:, row_idx[None, None, :, None], col_idx[:, :, None, :]].astype(jnp.float32)
        s = jnp.where(col_mask[:, :, None, :], s + bias, NEG_INF)
        p = jax.nn.softmax(s.reshape(B, NH, ncb, NA_Q_BLOCK_COLS, kr * NA_K_BLOCK_COLS), axis=-1)
        p = p.reshape(s.shape).astype(v.dtype)
        o = jnp.einsum('bhnqrk,brnkhd->bnqhd', p, v_blk)
        return o.reshape(B, GRID_W, NH, DH)

    out = lax.map(row_block, jnp.arange(rows, dtype=jnp.int32))
    return out.transpose(1, 0, 2, 3, 4).reshape(B, S, NH * DH)

def _token_mixing(u, w_in, decay_fwd, decay_bwd, rel_bias, w_ret_out, w_na_out, w_out, pos):
    B, S, _ = u.shape
    points = [sum(MIX_SPLITS[:i + 1]) for i in range(len(MIX_SPLITS) - 1)]
    rq, rk, rv, rg, nq, nk, nv, g_ret, g_na = jnp.split(u @ w_in, points, axis=-1)
    heads = lambda a, d: a.reshape(B, S, RET_HEADS, d).transpose(0, 2, 1, 3).astype(jnp.float32)
    q = _rotary(heads(rq, RET_QK_DIM), pos)
    k = _rotary(heads(rk, RET_QK_DIM), pos) * (RET_QK_DIM ** -0.5)
    y = _bidirectional_retention(q, k, heads(rv, RET_V_DIM), decay_fwd, decay_bwd)
    y = y * lax.rsqrt(jnp.mean(y * y, axis=-1, keepdims=True) + RMS_EPS)
    y = y.transpose(0, 2, 1, 3).reshape(B, S, RET_V_W).astype(u.dtype)
    y_ret = (jax.nn.silu(rg) * y) @ w_ret_out
    na_heads = lambda a: a.reshape(B, S, NA_HEADS, NA_HEAD_DIM)
    y_na = _neighborhood_attention(na_heads(nq), na_heads(nk), na_heads(nv), rel_bias) @ w_na_out
    merged = jax.nn.sigmoid(g_ret) * y_ret + jax.nn.sigmoid(g_na) * y_na
    return merged @ w_out

def first_inputs(seed: int = 0) -> dict:
    key = jax.random.key(seed)
    ks = jax.random.split(key, 20)
    f32 = jnp.float32

    def w(k, shape, fan_in):
        return jax.random.normal(k, (DEPTH,) + shape, f32) * (fan_in ** -0.5)

    def gain(k):
        return 1.0 + 0.05 * jax.random.normal(k, (DEPTH, D_MODEL), f32)

    gamma0 = 1.0 - 2.0 ** (-5.0 - np.arange(RET_HEADS, dtype=np.float32))
    logit0 = jnp.asarray(np.log(gamma0 / (1.0 - gamma0)), f32)
    return {
        "x": jax.random.normal(ks[0], (BATCH, SEQ, D_MODEL), f32),
        "ffn1_pre_norm": gain(ks[1]),
        "ffn1_w_in": w(ks[2], (D_MODEL, 2 * D_FF), D_MODEL),
        "ffn1_w_out": w(ks[3], (D_FF, D_MODEL), D_FF),
        "ffn1_post_norm": gain(ks[4]),
        "mix_pre_norm": gain(ks[5]),
        "w_mix_in": w(ks[6], (D_MODEL, MIX_IN_W), D_MODEL),
        "ret_decay_fwd": logit0[None] + 0.1 * jax.random.normal(ks[7], (DEPTH, RET_HEADS), f32),
        "ret_decay_bwd": logit0[None] + 0.1 * jax.random.normal(ks[8], (DEPTH, RET_HEADS), f32),
        "na_rel_bias": 0.02 * jax.random.normal(ks[9], (DEPTH, NA_HEADS, NA_REL_ROWS, NA_REL_COLS), f32),
        "w_ret_out": w(ks[10], (RET_V_W, D_MODEL), RET_V_W),
        "w_na_out": w(ks[11], (NA_W, D_MODEL), NA_W),
        "w_mix_out": w(ks[12], (D_MODEL, D_MODEL), D_MODEL),
        "mix_post_norm": gain(ks[13]),
        "ffn2_pre_norm": gain(ks[14]),
        "ffn2_w_in": w(ks[15], (D_MODEL, 2 * D_FF), D_MODEL),
        "ffn2_w_out": w(ks[16], (D_FF, D_MODEL), D_FF),
        "ffn2_post_norm": gain(ks[17]),
    }

def first_block(x, ffn1_pre_norm, ffn1_w_in, ffn1_w_out, ffn1_post_norm, mix_pre_norm, w_mix_in,
              ret_decay_fwd, ret_decay_bwd, na_rel_bias, w_ret_out, w_na_out, w_mix_out, mix_post_norm,
              ffn2_pre_norm, ffn2_w_in, ffn2_w_out, ffn2_post_norm):
    S = x.shape[1]
    pos = jnp.arange(S, dtype=jnp.float32)
    for l in range(DEPTH):
        h = _swiglu(_rms_norm(x, ffn1_pre_norm[l]), ffn1_w_in[l], ffn1_w_out[l])
        x = x + 0.5 * _rms_norm(h, ffn1_post_norm[l])
        m = _token_mixing(_rms_norm(x, mix_pre_norm[l]), w_mix_in[l], ret_decay_fwd[l], ret_decay_bwd[l],
                          na_rel_bias[l], w_ret_out[l], w_na_out[l], w_mix_out[l], pos)
        x = x + _rms_norm(m, mix_post_norm[l])
        h = _swiglu(_rms_norm(x, ffn2_pre_norm[l]), ffn2_w_in[l], ffn2_w_out[l])
        x = x + 0.5 * _rms_norm(h, ffn2_post_norm[l])
    return x


DEPTH_2 = 2

N_MIXERS = 2
N_MOBA_LAYERS = (DEPTH_2 + 1) // 2
N_DIFF_LAYERS = DEPTH_2 // 2
MOBA_HEAD_DIM = 64
MOBA_HEADS = D_MODEL // MOBA_HEAD_DIM
MOBA_BLOCK = 256
MOBA_TOPK = 3
MOBA_Q_CHUNK = 16
DIFF_HEAD_DIM = 64
DIFF_HEADS = D_MODEL // (2 * DIFF_HEAD_DIM)
DIFF_Q_BLOCK = 128
D_FF_2 = 4 * D_MODEL
ROPE_THETA = 500000.0
MOBA_ROT = MOBA_HEAD_DIM // 4
DIFF_ROT = DIFF_HEAD_DIM // 4
DEEPNORM_ALPHA = (2.0 * DEPTH_2) ** 0.25
DEEPNORM_BETA = (8.0 * DEPTH_2) ** -0.25
LN_EPS = 1e-5
SUBLN_EPS = 1e-5
ADA_SCALE = 0.1
NEG_INF_2 = -1e30


def rope_tables(seq_len, rot_dim):
    pos = jnp.arange(seq_len, dtype=jnp.float32)
    inv = ROPE_THETA ** (-jnp.arange(0, rot_dim, 2, dtype=jnp.float32) / rot_dim)
    ang = pos[:, None] * inv[None, :]
    return jnp.cos(ang), jnp.sin(ang)

def partial_rope(x, cos, sin):
    half = cos.shape[-1]
    x1, x2, xp = x[..., :half], x[..., half:2 * half], x[..., 2 * half:]
    c = cos.astype(x.dtype)
    s = sin.astype(x.dtype)
    return jnp.concatenate([x1 * c - x2 * s, x2 * c + x1 * s, xp], axis=-1)

def layer_norm(x, g, b):
    xf = x.astype(jnp.float32)
    mu = jnp.mean(xf, axis=-1, keepdims=True)
    var = jnp.mean(jnp.square(xf - mu), axis=-1, keepdims=True)
    return ((xf - mu) * lax.rsqrt(var + LN_EPS)).astype(x.dtype) * g + b

def rms_norm(x, g):
    xf = x.astype(jnp.float32)
    return (xf * lax.rsqrt(jnp.mean(jnp.square(xf), axis=-1, keepdims=True) + SUBLN_EPS)).astype(x.dtype) * g

def moba_attention(h, w_in, w_out):
    B, S, _ = h.shape
    H, hd, BLK, QC = MOBA_HEADS, MOBA_HEAD_DIM, MOBA_BLOCK, MOBA_Q_CHUNK
    cos, sin = rope_tables(S, MOBA_ROT)
    q, k, v = jnp.split(h @ w_in, 3, axis=-1)
    to_heads = lambda t: t.reshape(B, S, H, hd).transpose(0, 2, 1, 3)
    q = partial_rope(to_heads(q), cos, sin)
    k = partial_rope(to_heads(k), cos, sin)
    v = to_heads(v)
    nb = -(-S // BLK)
    pad = nb * BLK - S
    k_blocks = jnp.pad(k, ((0, 0), (0, 0), (0, pad), (0, 0))).reshape(B, H, nb, BLK, hd)
    v_blocks = jnp.pad(v, ((0, 0), (0, 0), (0, pad), (0, 0))).reshape(B, H, nb, BLK, hd)
    scale = hd ** -0.5
    q_block = jnp.arange(S) // BLK
    n_sel = min(MOBA_TOPK, nb - 1)
    nc = S // QC

    def chunk(t):
        return jnp.moveaxis(t.reshape(t.shape[:2] + (nc, QC) + t.shape[3:]), 2, 0)

    xs = {"q": chunk(q), "start": jnp.arange(nc, dtype=jnp.int32) * QC}
    if n_sel > 0:
        k_mean = jnp.mean(k_blocks.astype(jnp.float32), axis=3)
        gate = jnp.einsum('bhsd,bhnd->bhsn', q.astype(jnp.float32), k_mean)
        past = jnp.arange(nb)[None, :] < q_block[:, None]
        gate = jnp.where(past, gate, NEG_INF_2)
        _, sel_idx = lax.top_k(gate, n_sel)
        sel_valid = jnp.arange(n_sel)[None, :] < q_block[:, None]
        xs["idx"] = chunk(sel_idx)
        xs["valid"] = sel_valid.reshape(nc, QC, n_sel)
    b_ix = jnp.arange(B)[:, None, None, None]
    h_ix = jnp.arange(H)[None, :, None, None]

    def step(a):
        q_c, start = a["q"], a["start"]
        own = start // BLK
        k_own = lax.dynamic_index_in_dim(k_blocks, own, axis=2, keepdims=False)
        v_own = lax.dynamic_index_in_dim(v_blocks, own, axis=2, keepdims=False)
        q_pos = start + jnp.arange(QC)
        k_pos = own * BLK + jnp.arange(BLK)
        s_own = jnp.einsum('bhqd,bhkd->bhqk', q_c, k_own).astype(jnp.float32) * scale
        s_own = jnp.where(k_pos[None, :] <= q_pos[:, None], s_own, NEG_INF_2)
        if n_sel == 0:
            p = jax.nn.softmax(s_own, axis=-1).astype(v.dtype)
            return jnp.einsum('bhqk,bhkd->bhqd', p, v_own)
        idx_c = a["idx"]
        k_sel = k_blocks[b_ix, h_ix, idx_c]
        v_sel = v_blocks[b_ix, h_ix, idx_c]
        s_sel = jnp.einsum('bhqd,bhqnkd->bhqnk', q_c, k_sel).astype(jnp.float32) * scale
        s_sel = jnp.where(a["valid"][None, None, :, :, None], s_sel, NEG_INF_2)
        s_all = jnp.concatenate([s_own, s_sel.reshape(B, H, QC, n_sel * BLK)], axis=-1)
        p = jax.nn.softmax(s_all, axis=-1).astype(v.dtype)
        p_own = p[..., :BLK]
        p_sel = p[..., BLK:].reshape(B, H, QC, n_sel, BLK)
        return (jnp.einsum('bhqk,bhkd->bhqd', p_own, v_own)
                + jnp.einsum('bhqnk,bhqnkd->bhqd', p_sel, v_sel))

    o = lax.map(step, xs)
    o = jnp.moveaxis(o, 0, 2).reshape(B, H, S, hd)
    return o.transpose(0, 2, 1, 3).reshape(B, S, H * hd) @ w_out

def diff_attention(h, w_in, w_out, lam_q1, lam_k1, lam_q2, lam_k2, subln_g, lambda_init):
    B, S, _ = h.shape
    H, d, QB = DIFF_HEADS, DIFF_HEAD_DIM, DIFF_Q_BLOCK
    cos, sin = rope_tables(S, DIFF_ROT)
    q, k, v = jnp.split(h @ w_in, 3, axis=-1)
    q = partial_rope(q.reshape(B, S, H, 2, d).transpose(0, 2, 3, 1, 4), cos, sin)
    k = partial_rope(k.reshape(B, S, H, 2, d).transpose(0, 2, 3, 1, 4), cos, sin)
    v = v.reshape(B, S, H, 2 * d).transpose(0, 2, 1, 3)
    f32 = jnp.float32
    lam = (jnp.exp(jnp.sum(lam_q1.astype(f32) * lam_k1.astype(f32)))
           - jnp.exp(jnp.sum(lam_q2.astype(f32) * lam_k2.astype(f32))) + lambda_init)
    nqb = S // QB
    q_blocks = jnp.moveaxis(q.reshape(B, H, 2, nqb, QB, d), 3, 0)
    k_pos = jnp.arange(S)
    scale = d ** -0.5

    def step(a):
        q_b, start = a
        s = jnp.einsum('bhcqd,bhckd->bhcqk', q_b, k).astype(f32) * scale
        q_pos = start + jnp.arange(QB)
        s = jnp.where(k_pos[None, :] <= q_pos[:, None], s, NEG_INF_2)
        p = jax.nn.softmax(s, axis=-1)
        w = (p[:, :, 0] - lam * p[:, :, 1]).astype(v.dtype)
        return jnp.einsum('bhqk,bhke->bhqe', w, v)

    o = lax.map(step, (q_blocks, jnp.arange(nqb, dtype=jnp.int32) * QB))
    o = jnp.moveaxis(o, 0, 2).reshape(B, H, S, 2 * d)
    o = rms_norm(o, subln_g) * (1.0 - lambda_init)
    return o.transpose(0, 2, 1, 3).reshape(B, S, H * 2 * d) @ w_out

def sq_relu_mlp(h, w_up, w_down):
    return jnp.square(jax.nn.relu(h @ w_up)) @ w_down

def second_inputs(seed: int = 0) -> dict:
    key = jax.random.key(seed)
    ks = jax.random.split(key, 20)
    D = D_MODEL
    nrm = lambda k, shape: jax.random.normal(k, shape, dtype=jnp.float32)
    in_col_scale = jnp.concatenate([jnp.ones((2 * D,), jnp.float32),
                                    jnp.full((D,), DEEPNORM_BETA, jnp.float32)])
    return {
        "x": nrm(ks[0], (BATCH, SEQ, D)),
        "c": nrm(ks[1], (BATCH, D)),
        "moba_w_in": nrm(ks[2], (N_MOBA_LAYERS, D, 3 * D)) * D ** -0.5 * in_col_scale,
        "moba_w_out": nrm(ks[3], (N_MOBA_LAYERS, D, D)) * D ** -0.5 * DEEPNORM_BETA,
        "diff_w_in": nrm(ks[4], (N_DIFF_LAYERS, D, 3 * D)) * D ** -0.5 * in_col_scale,
        "diff_w_out": nrm(ks[5], (N_DIFF_LAYERS, D, D)) * D ** -0.5 * DEEPNORM_BETA,
        "diff_lam_q1": nrm(ks[6], (N_DIFF_LAYERS, DIFF_HEAD_DIM)) * 0.1,
        "diff_lam_k1": nrm(ks[7], (N_DIFF_LAYERS, DIFF_HEAD_DIM)) * 0.1,
        "diff_lam_q2": nrm(ks[8], (N_DIFF_LAYERS, DIFF_HEAD_DIM)) * 0.1,
        "diff_lam_k2": nrm(ks[9], (N_DIFF_LAYERS, DIFF_HEAD_DIM)) * 0.1,
        "diff_subln_g": 1.0 + 0.02 * nrm(ks[10], (N_DIFF_LAYERS, 2 * DIFF_HEAD_DIM)),
        "ada_w": nrm(ks[11], (DEPTH_2, D, 6 * D)) * D ** -0.5 * ADA_SCALE,
        "ada_b": 0.02 * nrm(ks[12], (DEPTH_2, 6 * D)),
        "ln_g": 1.0 + 0.02 * nrm(ks[13], (DEPTH_2, 2, D)),
        "ln_b": 0.02 * nrm(ks[14], (DEPTH_2, 2, D)),
        "mlp_w_up": nrm(ks[15], (DEPTH_2, D, D_FF_2)) * D ** -0.5,
        "mlp_w_down": nrm(ks[16], (DEPTH_2, D_FF_2, D)) * D_FF_2 ** -0.5 * DEEPNORM_BETA,
    }

def second_block(x, c, moba_w_in, moba_w_out, diff_w_in, diff_w_out, diff_lam_q1, diff_lam_k1,
              diff_lam_q2, diff_lam_k2, diff_subln_g, ada_w, ada_b, ln_g, ln_b, mlp_w_up, mlp_w_down):
    mod = jnp.einsum('bd,lde->lbe', jax.nn.silu(c), ada_w) + ada_b[:, None, :]
    for i in range(DEPTH_2):
        shift1, scale1, gate1, shift2, scale2, gate2 = [m[:, None, :] for m in jnp.split(mod[i], 6, axis=-1)]
        j = i // N_MIXERS
        h = x * (1.0 + scale1) + shift1
        if i % N_MIXERS == 0:
            y = moba_attention(h, moba_w_in[j], moba_w_out[j])
        else:
            lambda_init = 0.8 - 0.6 * math.exp(-0.3 * i)
            y = diff_attention(h, diff_w_in[j], diff_w_out[j], diff_lam_q1[j], diff_lam_k1[j],
                               diff_lam_q2[j], diff_lam_k2[j], diff_subln_g[j], lambda_init)
        x = layer_norm(DEEPNORM_ALPHA * x + (1.0 + gate1) * y, ln_g[i, 0], ln_b[i, 0])
        h = x * (1.0 + scale2) + shift2
        y = sq_relu_mlp(h, mlp_w_up[i], mlp_w_down[i])
        x = layer_norm(DEEPNORM_ALPHA * x + (1.0 + gate2) * y, ln_g[i, 1], ln_b[i, 1])
    return x


def setup_inputs(seed=0):
    out = dict(first_inputs(seed))
    for name, value in second_inputs(seed + 1).items():
        if name != "x":
            out[name + "_2"] = value
    return out


def reference(
    x, ffn1_pre_norm, ffn1_w_in, ffn1_w_out, ffn1_post_norm, mix_pre_norm, w_mix_in,
    ret_decay_fwd, ret_decay_bwd, na_rel_bias, w_ret_out, w_na_out, w_mix_out, mix_post_norm,
    ffn2_pre_norm, ffn2_w_in, ffn2_w_out, ffn2_post_norm, c_2, moba_w_in_2, moba_w_out_2,
    diff_w_in_2, diff_w_out_2, diff_lam_q1_2, diff_lam_k1_2, diff_lam_q2_2, diff_lam_k2_2,
    diff_subln_g_2, ada_w_2, ada_b_2, ln_g_2, ln_b_2, mlp_w_up_2, mlp_w_down_2,
):
    x = first_block(
        x, ffn1_pre_norm, ffn1_w_in, ffn1_w_out, ffn1_post_norm, mix_pre_norm, w_mix_in,
        ret_decay_fwd, ret_decay_bwd, na_rel_bias, w_ret_out, w_na_out, w_mix_out,
        mix_post_norm, ffn2_pre_norm, ffn2_w_in, ffn2_w_out, ffn2_post_norm,
    )
    return second_block(
        x, c_2, moba_w_in_2, moba_w_out_2, diff_w_in_2, diff_w_out_2, diff_lam_q1_2,
        diff_lam_k1_2, diff_lam_q2_2, diff_lam_k2_2, diff_subln_g_2, ada_w_2, ada_b_2, ln_g_2,
        ln_b_2, mlp_w_up_2, mlp_w_down_2,
    )


_drawn_inputs = setup_inputs


def setup_inputs(seed=0):
    import zlib

    import numpy as np

    out = dict(_drawn_inputs(seed))
    spreads = {}
    factors = {'na_rel_bias': 8.0,
     'ffn2_post_norm': 3.357,
     'diff_lam_q1_2': 5.783,
     'diff_lam_k1_2': 4.168,
     'diff_lam_k2_2': 3.695,
     'diff_subln_g_2': 8.0}
    for name, (base, spread) in spreads.items():
        noise = np.random.default_rng([zlib.crc32(name.encode()), seed]).standard_normal(out[name].shape)
        drawn = base * np.exp(spread * noise) if base else spread * noise
        out[name] = __import__('jax').numpy.asarray(drawn.astype(out[name].dtype))
    for name, factor in factors.items():
        out[name] = (out[name] * factor).astype(out[name].dtype)
    return out
```

```python
from contextlib import ExitStack
from dataclasses import dataclass
from typing import Any
import math

import numpy as np
import concourse.bass as bass
from concourse import mybir

ALU = mybir.AluOpType
ACT = mybir.ActivationFunctionType
AX = mybir.AxisListType
F32 = mybir.dt.float32
F32R = mybir.dt.float32r
U32 = mybir.dt.uint32
I32 = mybir.dt.int32

P = 128
SEQ = 256
NT = SEQ // P
D = 1024
KD = D // P
BANK = 512
D_FF = 2816
FF_B = 256
N_FF = D_FF // FF_B
D_MLP = 4096
MLP_B = 512
N_MLP = D_MLP // MLP_B
UNIT = 2048
RING = 4
AHEAD = 3
RET_H, RET_DK, RET_DV = 4, 128, 256
NA_H, NA_D = 8, 64
GRID = 64
REL_C = 31
GRID_R = SEQ // GRID
REL_USED = 2 * GRID_R - 1
ROT = 8
HD = 64
RMS_EPS, LN_EPS, SUBLN_EPS = 1e-6, 1e-5, 1e-5
ALPHA = 4.0 ** 0.25
LAMBDA_INIT = 0.8 - 0.6 * math.exp(-0.3)
NEG = -1e30
MIX_COLS = {"rq": 0, "rk": 512, "rv": 1024, "rg": 2048, "nq": 3072, "nk": 3584, "nv": 4096,
            "gr": 4608, "gn": 5632}
MIX_BLOCKS = [("rq", 0), ("rk", 0), ("nq", 0), ("nk", 0), ("rv", 0), ("rv", 1), ("nv", 0), ("rg", 0), ("rg", 1),
              ("gr", 0), ("gr", 1), ("gn", 0), ("gn", 1)]
N_MIX = len(MIX_BLOCKS)
QKV_BLOCKS = [("q", 0), ("k", 0), ("v", 0), ("q", 1), ("k", 1), ("v", 1)]
QKV_COL = {"q": 0, "k": D, "v": 2 * D}

U_FFN1 = 0
U_MIX = U_FFN1 + 3 * N_FF
U_FFN2 = U_MIX + 2 * N_MIX + 2 + 4 + 4
U_MOBA = U_FFN2 + 3 * N_FF
U_MLP1 = U_MOBA + 2 * len(QKV_BLOCKS) + 4
U_DIFF = U_MLP1 + 4 * N_MLP
U_MLP2 = U_DIFF + 2 * len(QKV_BLOCKS) + 4
N_UNITS = U_MLP2 + 4 * N_MLP
B_FFN1, B_FFN2 = 0, N_FF
B_MLP1 = 2 * N_FF
B_MLP2 = B_MLP1 + N_MLP
PB_MIX, PB_MOBA = 0, N_MIX
PB_DIFF = N_MIX + len(QKV_BLOCKS)
S_FFN1, S_MIX, S_FFN2, S_MOBA, S_MLP1, S_DIFF, S_MLP2 = range(7)
LAST_UNIT = {S_FFN1: U_MIX - 1, S_MIX: U_FFN2 - 1, S_FFN2: U_MOBA - 1, S_MOBA: U_MLP1 - 1, S_MLP1: U_DIFF - 1,
             S_DIFF: U_MLP2 - 1, S_MLP2: N_UNITS - 1}
CH_START = 0
CH_MIX = 8
CH_NA, CH_RET, CH_MERGED = 16, 20, 28
CH_FFN2, CH_MOBA = 36, 44
CH_MOBA_O, CH_MLP1, CH_DIFF, CH_DIFF_O, CH_MLP2 = 52, 60, 68, 76, 84
CH_AFTER = {-1: CH_START, S_FFN1: CH_MIX, S_MIX: CH_FFN2, S_FFN2: CH_MOBA, S_MOBA: CH_MLP1, S_MLP1: CH_DIFF,
            S_DIFF: CH_MLP2}
C_F1, C_MIX, C_F2, C_C, C_LNG, C_LNB = 0, 8, 16, 24, 32, 64
VEC_LOADS, VEC_LOADS_2, CONST_LOADS = 16 * 4, 16 * 3, 16 * 8
ATTENTION = [(0, [], []), (1, [], []), (2, [], ["H0"]), (3, [], []), (4, [], ["H1"]), (5, [], ["S0"]),
             (6, [], ["S1", "W0"]), (7, [], ["S2", "O0", "W1"]), (8, [], ["S3", "O1", "W2"]),
             (9, ["H2"], ["O2", "W3"]), (10, ["H3"], ["S4", "O3"]), (11, [], ["T0", "S5", "W4"]),
             (12, [], ["S6", "O4", "W5"]), (13, [], ["S7", "O5", "W6"]), (None, [], ["O6", "W7"]),
             (None, [], ["O7"]), (None, [], ["T1"]), (14, [], []), (15, [], [])]
N_PIECE = 24
LOOP_STEPS = 4


@dataclass
class Count:
    base: int
    per: int = 0
    turn: Any = None

    def __add__(self, n):
        return Count(self.base + n, self.per, self.turn)

    def value(self, scale=1, plus=0):
        v = self.base * scale + plus
        return v if self.turn is None else self.turn * (self.per * scale) + v

    def slot(self, ring=RING):
        assert self.turn is None or self.per % ring == 0
        return self.base % ring


class Steps:

    def __init__(self, sem):
        self.sem, self.n = sem, 0

    def inc(self, ins):
        ins.then_inc(self.sem, 1)
        self.n += 1

    def wait(self, eng):
        eng.wait_ge(self.sem, self.n)


def two_blocks_kernel(nc, d, out):
    with ExitStack() as ctx:
        def sb(name, shape, dt=F32):
            return ctx.enter_context(nc.sbuf_tensor(name, shape, dt))

        def sem(name):
            return ctx.enter_context(nc.semaphore(name))

        w_raw = sb("w_raw", [P, RING, UNIT])
        hi_w = sb("hi_w", [P, RING, UNIT], F32R)
        lo_w = sb("lo_w", [P, RING, UNIT], F32R)
        x = sb("x", [P, NT, D])
        xT_hi = sb("xT_hi", [P, KD, SEQ], F32R)
        xT_lo = sb("xT_lo", [P, KD, SEQ], F32R)
        hT_hi = sb("hT_hi", [P, 4, SEQ], F32R)
        hT_lo = sb("hT_lo", [P, 4, SEQ], F32R)
        aux = sb("aux", [P, 4096])
        piece_acc = sb("piece_acc", [P, 2, BANK])
        area = sb("area", [P, 13824])
        ident = sb("ident", [P, P])
        ones = sb("ones", [P, P])
        vec_cols = sb("vec_cols", [P, 96])
        adab_cols = sb("adab_cols", [P, 96])
        mod_cols = sb("mod_cols", [P, 96])
        c_act = sb("c_act", [P, KD])
        aff_a = sb("aff_a", [P, 4, KD])
        aff_b = sb("aff_b", [P, 4, KD])
        decay = sb("decay", [P, 2 * RET_H])
        dk = sb("dk", [P, 6, 2 * RET_H])
        lam_in = sb("lam_in", [P, 4, HD])
        lam = sb("lam", [P, 4])
        lam_prod = sb("lam_prod", [P, HD])
        subln = sb("subln", [P, P])
        na_mask = sb("na_mask", [P, GRID])
        sq = sb("sq", [P, NT])
        rstd = sb("rstd", [P, NT])
        sq_x = sb("sq_x", [P, NT])
        rstd_x = sb("rstd_x", [P, NT])
        newton = sb("newton", [P, 4, 4 * NT])
        moments = sb("moments", [P, NT, 2])
        head_sq = sb("head_sq", [P, 4, NT])
        head_rstd = sb("head_rstd", [P, 4 * NT])
        shift = sb("shift", [P, 1])
        top = sb("top", [P, 2, NT])
        total = sb("total", [P, 2, 4])
        inv = sb("inv", [P, 4])
        bst = sb("bst", [P, NT, 2, 6])
        rel_dram = nc.dram_tensor("rel_scratch", (REL_USED * NA_H, GRID * P), F32, kind="Internal").ap()
        mod_dram = nc.dram_tensor("mod_scratch", (96, P), F32, kind="Internal").ap()
        ps = ctx.enter_context(nc.psum_tensor("ps", [P, 8 * BANK], F32))

        def bank(b, n=1):
            return ps[:, b * BANK:(b + n) * BANK]

        def part(off, n, t=None):
            v = area[:, off:off + n]
            return v if t is None else v.rearrange("p (t n) -> p t n", t=t)

        act_s = part(0, NT * MLP_B, NT)
        hid = part(1024, NT * MLP_B, NT)
        zt = part(2048, NT * D, NT)
        qT = part(0, 1024, 4)
        kT = part(1024, 1024, 4)
        g_ret = part(0, 2048, NT)
        v_nat = part(2048, 2048, NT)
        g_na = v_nat
        nqT = part(4096, 1024, 4)
        nkT = part(5120, 1024, 4)
        nv = part(6144, 1024, NT)
        y_nat = part(7168, 2048, NT)
        silu_rg = [part(0, 1024, NT), part(1024, 1024, NT)]
        stage = [part(7168, 1024, NT), part(8192, 1024, NT)]
        nao = part(9216, 1024, NT)
        bias = [part(10240, 512, NT), part(10752, 512, NT)]
        scr = [part(11264 + 512 * i, 512) for i in range(5)]
        ret_probs, decays = scr[0:2], scr[2:4]
        decay_tmp = scr[4]
        na_scores, na_probs, na_probsT = scr[0], scr[1:3], scr[3:5]
        q2T = [part(0, 1024, 4), part(1024, 1024, 4)]
        k2T = [part(2048, 1024, 4), part(3072, 1024, 4)]
        v2 = part(4096, 2048, NT)
        stage2 = [part(6144, 1024, NT), part(7168, 1024, NT)]
        o2 = part(8192, 2048, NT)
        probs = part(10240, 768)
        probs_w = part(11008, 384)
        rope2_t = [part(11392 + 128 * i, 128, NT) for i in range(4)]
        probsT = part(11904, 768)
        causal = part(12672, 3 * P)
        rot2 = part(13056, 4 * 8 * ROT).rearrange("p (c t n) -> p c t n", c=2, t=NT)
        vec_rows, adab_rows = area[0:96, 0:P], area[0:96, P:2 * P]
        rel = area[0:REL_USED * NA_H, 11264 - P:11264]
        mod_rows = piece_acc[0:96, 0, 0:P]
        row_a, row_g, row_b = (aux[:, i * D:(i + 1) * D] for i in range(3))
        relu_t = [aux[:, 1024 + 512 * i:1536 + 512 * i] for i in range(2)]
        rot1 = aux[:, 2048:2304].rearrange("p (c t n) -> p c t n", c=2, t=NT)
        rope1_t = [aux[:, 2304 + 256 * i:2560 + 256 * i] for i in range(4)]
        row_ffn = part(12288, D)
        squares_of = aux[:, 3584:4096].rearrange("p (t n) -> p t n", t=NT)
        affine = [aux[:, 3072 + SEQ * i:3072 + SEQ * (i + 1)] for i in range(2)]

        w_landed = [sem(f"w_landed{i}") for i in range(RING)]
        w_hi, w_lo, w_used = sem("w_hi"), sem("w_lo"), sem("w_used")
        act_done, hid_done = sem("act_done"), sem("hid_done")
        hidT, hidT_hi, hidT_lo = sem("hidT"), sem("hidT_hi"), sem("hidT_lo")
        tile0_done = sem("tile0_done")
        sq_done = sem("sq_done")
        norm_done = [sem("norm_done0"), sem("norm_done1")]
        shift_done = sem("shift_done")
        chunksT = sem("chunksT")
        ch_act, ch_lo = sem("ch_act"), sem("ch_lo")
        x_new = sem("x_new")
        xsq_done, rstd_x_done = sem("xsq_done"), sem("rstd_x_done")
        proj_out = sem("proj_out")
        rot_done, headT, headT_out = sem("rot_done"), sem("headT"), sem("headT_out")
        mod_landed = [sem("mod_landed0"), sem("mod_landed1")]
        mod_step = sem("mod_step")
        piece_cols, piece_out = sem("piece_cols"), sem("piece_out")
        vec_step, pool_step = sem("vec_step"), sem("pool_step")
        ld_x, ld_vec, ld_vec2, ld_const, ld_row, ld_tab = sem("ld_x"), sem("ld_vec"), sem("ld_vec2"), sem("ld_const"), sem("ld_row"), sem("ld_tab")
        ones_set = sem("ones_set")
        vecT, vec_out, c_done = sem("vecT"), sem("vec_out"), sem("c_done")
        small_exp, small_in = sem("small_exp"), sem("small_in")
        exponent_done, decay_done = sem("exponent_done"), sem("decay_done")
        ret_s, ret_p, ret_y, ret_sq, ret_out = (sem("ret_" + n) for n in ("scores", "probs", "sums", "squares", "out"))
        gate_rg, gated, half_merged, merged = sem("gate_rg"), sem("gated"), sem("half_merged"), sem("merged")
        rel_zero, rel_in, rel_out, bias_in, bias_done = (
            sem(n) for n in ("rel_zero", "rel_in", "rel_out", "bias_in", "bias_done"))
        at_s, at_m, at_e, at_w, at_t, at_p, at_sq, at_o, at_out = (
            sem("at_" + n) for n in ("scores", "max", "exp", "weights", "weightsT", "weightsT_out", "squares",
                                     "outputs", "outputs_out"))
        mod_fin, mod_T, mod_row, mod_st = sem("mod_fin"), sem("mod_T"), sem("mod_row"), sem("mod_st")
        x_fin, stored = sem("x_fin"), sem("stored")

        block = ctx.enter_context(nc.Block())

        def chunk_off(s, k):
            if s in (S_FFN1, S_FFN2, S_MLP1):
                return (6, 0)[k // 4] * BANK + (k % 4) * SEQ
            return k * SEQ

        @block.sync
        def _(sp):
            def slot_free(u):
                if u.turn is not None or u.base >= RING:
                    sp.wait_ge(w_lo, u.value(1, 1 - RING))

            def unit(u, src, k):
                slot_free(u)
                dst = w_raw[:, u.slot(), :].rearrange("p (k n) -> p k n", k=k)
                sp.dma_start(dst, src).then_inc(w_landed[u.slot()], 32)

            def swiglu_in(u, w, i, half):
                slot_free(u)
                dst = w_raw[:, u.slot(), :].rearrange("p (k g f) -> p k g f", k=4, g=2)
                for g in range(2):
                    src = w[:, 4 * half:4 * half + 4, g, bass.ds(i.value(FF_B), FF_B)]
                    sp.dma_start(dst[:, :, g, :], src).then_inc(w_landed[u.slot()], 16)

            def swiglu(u0, w_in, w_out):
                w_in = w_in.rearrange("(k p) (g f) -> p k g f", p=P, g=2)
                w_out = w_out.rearrange("(b k p) n -> p b k n", p=P, k=2)

                def out_unit(u, i):
                    slot_free(u)
                    dst = w_raw[:, u.slot(), :].rearrange("p (k n) -> p k n", k=2)
                    src = w_out[:, bass.ds(i.value(), 1), :, :].rearrange("p b k n -> p (b k) n")
                    sp.dma_start(dst, src).then_inc(w_landed[u.slot()], 32)

                def step(u, i):
                    swiglu_in(u, w_in, i + 1, 0)
                    swiglu_in(u + 1, w_in, i + 1, 1)
                    out_unit(u + 2, i)

                swiglu_in(Count(u0), w_in, Count(0), 0)
                swiglu_in(Count(u0 + 1), w_in, Count(0), 1)
                for i in range(2):
                    step(Count(u0 + 2 + 3 * i), Count(i))
                with sp.Fori(0, (N_FF - 3) // LOOP_STEPS) as turn:
                    for j in range(LOOP_STEPS):
                        step(Count(u0 + 8 + 3 * j, 3 * LOOP_STEPS, turn), Count(2 + j, LOOP_STEPS, turn))
                out_unit(Count(u0 + 3 * N_FF - 1), Count(N_FF - 1))

            def mlp(u0, layer):
                w_up = d["mlp_w_up_2"][layer].rearrange("(k p) f -> p k f", p=P)
                w_dn = d["mlp_w_down_2"][layer].rearrange("(b k p) n -> p b k n", p=P, k=2)

                def up(u, i, half):
                    unit(u, w_up[:, 4 * half:4 * half + 4, bass.ds(i.value(MLP_B), MLP_B)], 4)

                def down(u, i, half):
                    src = w_dn[:, bass.ds(i.value(2, half), 1), :, :].rearrange("p b k n -> p (b k) n")
                    unit(u, src, 2)

                def step(u, i):
                    up(u, i + 1, 0)
                    up(u + 1, i + 1, 1)
                    down(u + 2, i, 0)
                    down(u + 3, i, 1)

                up(Count(u0), Count(0), 0)
                up(Count(u0 + 1), Count(0), 1)
                step(Count(u0 + 2), Count(0))
                with sp.Fori(0, (N_MLP - 2) // 2) as turn:
                    for j in range(2):
                        step(Count(u0 + 6 + 4 * j, 8, turn), Count(1 + j, 2, turn))
                for half in range(2):
                    down(Count(u0 + 4 * N_MLP - 2 + half), Count(N_MLP - 1), half)

            def square(u, w, n, half):
                unit(Count(u), w[:, 4 * half:4 * half + 4, n * BANK:(n + 1) * BANK], 4)

            def qkv_out(u0, w_in, w_out):
                w_in = w_in.rearrange("(k p) n -> p k n", p=P)
                w_out = w_out.rearrange("(k p) n -> p k n", p=P)
                for b, (name, j) in enumerate(QKV_BLOCKS):
                    for half in range(2):
                        square(u0 + 2 * b + half, w_in, QKV_COL[name] // BANK + j, half)
                for i in range(4):
                    square(u0 + 2 * len(QKV_BLOCKS) + i, w_out, i % 2, i // 2)

            sp.dma_start(ident[:, :], d["ident"]).then_inc(ld_x, 16)
            for t in range(NT):
                sp.dma_start(x[:, t, :], d["x"][0, t * P:(t + 1) * P, :]).then_inc(ld_x, 16)
            swiglu(U_FFN1, d["ffn1_w_in"][0], d["ffn1_w_out"][0])
            w_mix = d["w_mix_in"][0].rearrange("(k p) n -> p k n", p=P)
            for b, (name, j) in enumerate(MIX_BLOCKS):
                for half in range(2):
                    square(U_MIX + 2 * b + half, w_mix, MIX_COLS[name] // BANK + j, half)
            u = U_MIX + 2 * N_MIX
            w_na = d["w_na_out"][0].rearrange("(k p) n -> p k n", p=P)
            w_ret = d["w_ret_out"][0].rearrange("(k p) n -> p k n", p=P)
            w_mo = d["w_mix_out"][0].rearrange("(k p) n -> p k n", p=P)
            for n in range(2):
                square(u + n, w_na, n, 0)
            for n in range(2):
                for half in range(2):
                    square(u + 2 + 2 * n + half, w_ret, n, half)
            for i in range(4):
                square(u + 6 + i, w_mo, i % 2, i // 2)
            swiglu(U_FFN2, d["ffn2_w_in"][0], d["ffn2_w_out"][0])
            qkv_out(U_MOBA, d["moba_w_in_2"][0], d["moba_w_out_2"][0])
            mlp(U_MLP1, 0)
            qkv_out(U_DIFF, d["diff_w_in_2"][0], d["diff_w_out_2"][0])
            mlp(U_MLP2, 1)
            for t in range(NT):
                sp.wait_ge(x_fin, t + 1)
                sp.dma_start(out[0, t * P:(t + 1) * P, :], x[:, t, :]).then_inc(stored, 16)
            sp.wait_ge(stored, 16 * NT)

        @block.tensor
        def _(pe):
            def three(dst, lhs_hi, lhs_lo, rhs_hi, rhs_lo, start, stop):
                pe.matmul(dst, lhs_hi, rhs_hi, start=start, stop=False)
                pe.matmul(dst, lhs_lo, rhs_hi, start=False, stop=False)
                return pe.matmul(dst, lhs_hi, rhs_lo, start=False, stop=stop)

            def in_unit(u, lhs, c0, banks, first, last, ch=None, tile0=False, tiles=range(NT)):
                pe.wait_ge(w_lo, u.value(1, 1))
                rhi = hi_w[:, u.slot(), :].rearrange("p (k n) -> p k n", k=4)
                rlo = lo_w[:, u.slot(), :].rearrange("p (k n) -> p k n", k=4)
                for t in tiles:
                    tok = slice(t * P, (t + 1) * P)
                    for k in range(4):
                        c = c0 + k
                        if t == 0 and ch is not None:
                            pe.wait_ge(ch_lo, ch + c + 1)
                        mm = three(bank(banks[t]), lhs[0][:, c, tok], lhs[1][:, c, tok], rhi[:, k, :],
                                   rlo[:, k, :], first and k == 0, last and k == 3)
                    if t == NT - 1:
                        mm.then_inc(w_used, 1)
                    elif tile0:
                        mm.then_inc(tile0_done, 1)

            def down_unit(u, c0, first, last, tile0=False, tiles=range(NT)):
                pe.wait_ge(w_lo, u.value(1, 1))
                rhi = hi_w[:, u.slot(), :].rearrange("p (k n) -> p k n", k=2)
                rlo = lo_w[:, u.slot(), :].rearrange("p (k n) -> p k n", k=2)
                for t in tiles:
                    tok = slice(t * P, (t + 1) * P)
                    for n in range(2):
                        col = slice(n * BANK, (n + 1) * BANK)
                        for k in range(2):
                            mm = three(bank(2 * t + n), hT_hi[:, c0 + k, tok], hT_lo[:, c0 + k, tok],
                                       rhi[:, k, col], rlo[:, k, col], first and k == 0, last and k == 1)
                    if t == NT - 1:
                        mm.then_inc(w_used, 1)
                    elif tile0:
                        mm.then_inc(tile0_done, 1)

            def transposes(src, col0, n, off0):
                for c in range(n):
                    for t in range(NT):
                        off = off0 + c * SEQ + t * P
                        mm = pe.transpose(ps[:, off:off + P], src[:, t, col0 + c * P:col0 + (c + 1) * P], ident[:, :])
                return mm

            def x_chunks(s, src):
                if src is zt:
                    for t in range(NT):
                        pe.wait_ge(norm_done[t], s + 1)
                    chunks_of(src, 0, KD, chunk_off(s, 0), chunk_off(s, 4))
                    return
                for t in range(NT):
                    if s >= 0:
                        pe.wait_ge(norm_done[t], s + 1)
                    for k in range(KD):
                        off = chunk_off(s, k) + t * P
                        mm = pe.transpose(ps[:, off:off + P], src[:, t, k * P:(k + 1) * P], ident[:, :])
                        if t == NT - 1:
                            mm.then_inc(chunksT, 1)

            def chunks_of(src, col0, n, off0, off4=None):
                for c in range(n):
                    off = off0 + c * SEQ if off4 is None or c < 4 else off4 + (c - 4) * SEQ
                    transposes(src, col0 + c * P, 1, off).then_inc(chunksT, 1)

            def hidden_T(b, i, chunks):
                pe.wait_ge(hid_done, b.value(1, 1))
                transposes(hid, 0, chunks, (4 + 2 * (i % 2)) * BANK).then_inc(hidT, 1)

            def pair_free(b):
                pe.wait_ge(hidT_hi, b.value(1, -1))
                pe.wait_ge(hidT_lo, b.value(1, -1))

            def piece_columns(p, i, col):
                pe.wait_ge(mod_step, p.value(KD, KD))
                for j in range(4):
                    off = (5 + 2 * (i % 2)) * BANK + col + j
                    mm = pe.matmul(ps[:, off:off + 1], piece_acc[:, p.slot(2), j * P:(j + 1) * P], ones[:, 0:1],
                                   start=True, stop=True)
                mm.then_inc(piece_cols, 1)

            xT = (xT_hi, xT_lo)
            hT = (hT_hi, hT_lo)

            def swiglu(u0, b0, p0, ch):
                def gate_up(u, b, i, half, ch=None, busy=True):
                    if half == 0 and busy:
                        pair_free(b)
                        pe.wait_ge(piece_out, (b + (p0 - b0 - 1)).value())
                    pair = 4 + 2 * (i % 2)
                    in_unit(u, xT, 4 * half, [pair, pair + 1], half == 0, half == 1, ch)

                def step(u, b, i, first=False):
                    gate_up(u, b + 1, i + 1, 0, busy=not first)
                    hidden_T(b, i, 2)
                    piece_columns(b + (p0 - b0), i, 0)
                    gate_up(u + 1, b + 1, i + 1, 1)
                    pe.wait_ge(hidT_lo, b.value(1, 1))
                    down_unit(u + 2, 0, first, False)

                for half in range(2):
                    gate_up(Count(u0 + half), Count(b0), 0, half, ch, busy=False)
                for i in range(2):
                    step(Count(u0 + 2 + 3 * i), Count(b0 + i), i, first=i == 0)
                with pe.Fori(0, (N_FF - 3) // LOOP_STEPS) as turn:
                    for j in range(LOOP_STEPS):
                        step(Count(u0 + 8 + 3 * j, 3 * LOOP_STEPS, turn), Count(b0 + 2 + j, LOOP_STEPS, turn), 2 + j)
                last = Count(b0 + N_FF - 1)
                hidden_T(last, N_FF - 1, 2)
                piece_columns(Count(p0 + N_FF - 1), N_FF - 1, 0)
                pe.wait_ge(hidT_lo, last.value(1, 1))
                down_unit(Count(u0 + 3 * N_FF - 1), 0, False, True, tile0=True)
                pe.wait_ge(piece_out, p0 + N_FF)
                piece_columns(Count(p0 + N_FF), N_FF - 1, 4)
                pe.wait_ge(piece_out, p0 + N_FF + 1)

            def mlp(u0, b0, ch):
                def up(u, b, i, half, ch=None, busy=True):
                    if half == 0 and busy:
                        pair_free(b)
                    pair = 4 + 2 * (i % 2)
                    in_unit(u, xT, 4 * half, [pair, pair + 1], half == 0, half == 1, ch)

                def step(u, b, i, first=False):
                    up(u, b + 1, i + 1, 0, busy=not first)
                    hidden_T(b, i, 4)
                    up(u + 1, b + 1, i + 1, 1)
                    pe.wait_ge(hidT_lo, b.value(1, 1))
                    down_unit(u + 2, 0, first, False)
                    down_unit(u + 3, 2, False, False)

                for half in range(2):
                    up(Count(u0 + half), Count(b0), 0, half, ch, busy=False)
                step(Count(u0 + 2), Count(b0), 0, first=True)
                with pe.Fori(0, (N_MLP - 2) // 2) as turn:
                    for j in range(2):
                        step(Count(u0 + 6 + 4 * j, 8, turn), Count(b0 + 1 + j, 2, turn), 1 + j)
                last = Count(b0 + N_MLP - 1)
                hidden_T(last, N_MLP - 1, 4)
                pe.wait_ge(hidT_lo, last.value(1, 1))
                for t in range(NT):
                    down_unit(Count(u0 + 4 * N_MLP - 2), 0, False, False, tiles=[t])
                    down_unit(Count(u0 + 4 * N_MLP - 1), 2, False, True, tile0=True, tiles=[t])

            def proj(u0, pb, b, half, ch, tiles=range(NT)):
                if b >= 2 and half == 0 and 0 in tiles:
                    pe.wait_ge(proj_out, pb + b - 1)
                pair = 4 + 2 * (b % 2)
                in_unit(Count(u0 + 2 * b + half), xT, 4 * half, [pair, pair + 1], half == 0, half == 1,
                        ch if b == 0 else None, tiles=tiles)

            pe.wait_ge(ld_x, 16 * (NT + 1))
            x_chunks(-1, x)
            pe.wait_ge(ld_vec, VEC_LOADS)
            pe.wait_ge(ld_vec2, VEC_LOADS_2)
            pe.transpose(ps[:, 6 * BANK:6 * BANK + 96], vec_rows[:, :], ident[0:96, 0:96])
            pe.transpose(ps[:, 7 * BANK:7 * BANK + 96], adab_rows[:, :], ident[0:96, 0:96]).then_inc(vecT, 1)
            pe.wait_ge(vec_out, 1)
            pe.wait_ge(ones_set, 1)
            swiglu(U_FFN1, B_FFN1, 0, CH_START)

            x_chunks(S_FFN1, x)

            def ret_scores(h):
                pe.wait_ge(headT_out, 3)
                if h >= 2:
                    pe.wait_ge(ret_p, h - 1)
                for m in range(NT):
                    off = (h % 2) * BANK + m * SEQ
                    mm = pe.matmul(ps[:, off:off + SEQ], kT[:, h, m * P:(m + 1) * P], qT[:, h, :],
                                   start=True, stop=True)
                mm.then_inc(ret_s, 1)

            def ret_outputs(h):
                pe.wait_ge(ret_p, h + 1)
                pe.wait_ge(proj_out, PB_MIX + 5 + h // 2)
                pe.wait_ge(headT_out, 4)
                if h >= 2:
                    pe.wait_ge(ret_out, h - 1)
                for t in range(NT):
                    for m in range(NT):
                        off = (2 + h % 2) * BANK + t * RET_DV
                        mm = pe.matmul(ps[:, off:off + RET_DV],
                                       ret_probs[h % 2][:, m * SEQ + t * P:m * SEQ + (t + 1) * P],
                                       v_nat[:, m, h * RET_DV:(h + 1) * RET_DV], start=m == 0, stop=m == NT - 1)
                mm.then_inc(ret_y, 1)

            def na_scores_of(h):
                pe.wait_ge(headT_out, 4)
                pe.wait_ge(ret_p, RET_H)
                if h >= 2:
                    pe.wait_ge(at_m, h - 1)
                row = slice(NA_D * (h % 2), NA_D * (h % 2) + NA_D)
                for t in range(NT):
                    off = (h % 2) * BANK + t * SEQ
                    mm = pe.matmul(ps[:, off:off + SEQ], nqT[row, h // 2, t * P:(t + 1) * P], nkT[row, h // 2, :],
                                   start=True, stop=True)
                mm.then_inc(at_s, 1)

            def na_weights_T(h):
                pe.wait_ge(at_e, h + 1)
                pe.wait_ge(ret_out, RET_H)
                if h >= 1:
                    pe.wait_ge(at_p, h)
                for m in range(NT):
                    for t in range(NT):
                        off = 2 * BANK + m * SEQ + t * P
                        src = na_probs[h % 2][:, t * SEQ + m * P:t * SEQ + (m + 1) * P]
                        mm = pe.transpose(ps[:, off:off + P], src, ident[:, :])
                mm.then_inc(at_t, 1)

            def na_outputs(h):
                pe.wait_ge(at_p, h + 1)
                pe.wait_ge(proj_out, PB_MIX + 7)
                if h >= 1:
                    pe.wait_ge(at_out, h)
                for t in range(NT):
                    for m in range(NT):
                        off = 3 * BANK + t * NA_D
                        mm = pe.matmul(ps[:, off:off + NA_D],
                                       na_probsT[h % 2][:, m * SEQ + t * P:m * SEQ + (t + 1) * P],
                                       nv[:, m, h * NA_D:(h + 1) * NA_D], start=m == 0, stop=m == NT - 1)
                mm.then_inc(at_o, 1)

            for b in range(N_MIX):
                for half in range(2):
                    proj(U_MIX, PB_MIX, b, half, CH_MIX)
                    slot = 2 * b + half
                    if half == 1 and 1 <= b <= 4:
                        n = b - 1
                        if n < 2:
                            pe.wait_ge(rot_done, n + 1)
                        else:
                            pe.wait_ge(proj_out, PB_MIX + n + 1)
                            pe.wait_ge(headT_out, n - 1)
                        transposes(stage[n % 2], 0, 4, 2 * (n % 2) * BANK).then_inc(headT, 1)
                    if 0 <= slot - 10 < RET_H:
                        ret_outputs(slot - 10)
                    if 0 <= slot - 8 < RET_H:
                        ret_scores(slot - 8)
                    if 0 <= slot - 16 < NA_H:
                        na_outputs(slot - 16)
                    if 0 <= slot - 15 < NA_H:
                        na_weights_T(slot - 15)
                    if 0 <= slot - 14 < NA_H:
                        na_scores_of(slot - 14)
                    if slot == 24:
                        pe.wait_ge(at_out, NA_H)
                        pe.wait_ge(proj_out, PB_MIX + 12)
                        chunks_of(nao, 0, 4, 6 * BANK)
            pe.wait_ge(gated, 2)
            pe.wait_ge(at_p, NA_H)
            chunks_of(y_nat, 0, KD, 0)
            u = U_MIX + 2 * N_MIX
            for n in range(2):
                if n == 0:
                    pe.wait_ge(ch_lo, CH_NA + 4)
                else:
                    pe.wait_ge(proj_out, PB_MIX + N_MIX)
                pair = 6 - 2 * n
                in_unit(Count(u + n), hT, 0, [pair, pair + 1], True, True)
            pe.wait_ge(ch_lo, CH_RET + KD)
            for half in range(2):
                in_unit(Count(u + 2 + half), xT, 4 * half, [0, 1], half == 0, half == 1)
            in_unit(Count(u + 4), xT, 0, [2, 3], True, False)
            pe.wait_ge(merged, 1)
            chunks_of(g_ret, 0, 4, 6 * BANK)
            in_unit(Count(u + 5), xT, 4, [2, 3], False, True)
            pe.wait_ge(half_merged, 2)
            for n in range(2):
                if n == 0:
                    pe.wait_ge(ch_lo, CH_MERGED + 4)
                in_unit(Count(u + 6 + n), hT, 0, [4 + n, 6 + n], True, False)
            pe.wait_ge(merged, 2)
            chunks_of(g_ret, BANK, 4, 0)
            for n in range(2):
                in_unit(Count(u + 8 + n), xT, 4, [4 + n, 6 + n], False, True, CH_MERGED, tile0=n == 1)
            x_chunks(S_MIX, x)
            swiglu(U_FFN2, B_FFN2, N_PIECE // 2, CH_FFN2)

            x_chunks(S_FFN2, x)
            pe.wait_ge(mod_fin, 1)
            pe.transpose(ps[0:96, 4 * BANK:4 * BANK + P], mod_cols[:, :], ident[:, :]).then_inc(mod_T, 1)
            pe.wait_ge(mod_row, 1)

            def attention(u0, pb, hb, ab, ch, ch_o, diff):
                def heads_T(n):
                    pe.wait_ge(rot_done, hb - 2 + n + 1)
                    if n >= 1:
                        pe.wait_ge(headT_out, hb + n)
                    if n >= 2:
                        pe.wait_ge(at_m, ab + 4)
                    transposes(stage2[n % 2], 0, 4, 0).then_inc(headT, 1)

                def scores(c):
                    half, j = c // 4, c % 4
                    pe.wait_ge(headT_out, hb + 2 * half + 2)
                    pe.wait_ge(at_m, ab + c)
                    for e in range(2):
                        row = slice(HD * e, HD * e + HD)
                        pe.matmul(ps[:, e * BANK:e * BANK + P], q2T[half][row, j, 0:P], k2T[half][row, j, 0:P],
                                  start=True, stop=True)
                        mm = pe.matmul(ps[:, e * BANK + P:e * BANK + 3 * P], q2T[half][row, j, P:SEQ],
                                       k2T[half][row, j, :], start=True, stop=True)
                    mm.then_inc(at_s, 1)

                def weights_T(c):
                    if diff:
                        pe.wait_ge(at_w, c + 1)
                    else:
                        pe.wait_ge(at_e, ab + c + 1)
                    pe.wait_ge(at_p, ab + c)
                    if c % 4 == 0:
                        pe.wait_ge(at_out, ab + c)
                    src, n = (probs_w, 3) if diff else (probs, 6)
                    for j in range(n):
                        off = 2 * BANK + j * P
                        mm = pe.transpose(ps[:, off:off + P], src[:, j * P:(j + 1) * P], ident[:, :])
                    mm.then_inc(at_t, 1)

                def outputs(c):
                    pe.wait_ge(at_p, ab + c + 1)
                    pe.wait_ge(at_out, ab + c)
                    pe.wait_ge(proj_out, pb + 3 * (c // 4) + 3)
                    n_e, width = (1, 2 * HD) if diff else (2, HD)
                    for e in range(n_e):
                        pT = probsT[:, e * 3 * P:(e + 1) * 3 * P]
                        col = slice(c * P + e * HD, c * P + e * HD + width)
                        off = 3 * BANK + SEQ + e * 2 * HD
                        pe.matmul(ps[:, off:off + width], pT[:, 0:P], v2[:, 0, col], start=True, stop=True)
                        pe.matmul(ps[:, off + width:off + 2 * width], pT[:, P:2 * P], v2[:, 0, col],
                                  start=True, stop=False)
                        mm = pe.matmul(ps[:, off + width:off + 2 * width], pT[:, 2 * P:3 * P], v2[:, 1, col],
                                       start=False, stop=True)
                    mm.then_inc(at_o, 1)

                def outputs_T(half):
                    pe.wait_ge(at_out, ab + 4 * half + 4)
                    if half == 0:
                        pe.wait_ge(proj_out, pb + 5)
                    else:
                        pe.wait_ge(at_m, ab + 8)
                    chunks_of(o2, half * BANK, 4, 4 * BANK if half == 0 else 0)

                do = {"H": heads_T, "S": scores, "W": weights_T, "O": outputs, "T": outputs_T}
                for slot, between, events in ATTENTION:
                    if slot is not None and slot < 12:
                        if not between:
                            proj(u0, pb, slot // 2, slot % 2, ch)
                        else:
                            proj(u0, pb, slot // 2, slot % 2, ch, tiles=[0])
                            for event in between:
                                do[event[0]](int(event[1:]))
                            proj(u0, pb, slot // 2, slot % 2, ch, tiles=[1])
                    elif slot in (12, 13):
                        n = slot - 12
                        if slot == 12:
                            pe.wait_ge(proj_out, pb + 6)
                            pe.wait_ge(ch_lo, ch_o + 4)
                        in_unit(Count(u0 + slot), xT, 0, [4 + n, 6 + n], True, False, ch_o)
                    elif slot == 14:
                        for t in range(NT):
                            for n in range(2):
                                in_unit(Count(u0 + slot + n), xT, 4, [4 + n, 6 + n], False, True, ch_o,
                                        tile0=n == 1, tiles=[t])
                    for event in events:
                        do[event[0]](int(event[1:]))

            attention(U_MOBA, PB_MOBA, 4, NA_H, CH_MOBA, CH_MOBA_O, False)
            x_chunks(S_MOBA, zt)
            mlp(U_MLP1, B_MLP1, CH_MLP1)
            x_chunks(S_MLP1, zt)
            attention(U_DIFF, PB_DIFF, 8, NA_H + 8, CH_DIFF, CH_DIFF_O, True)
            x_chunks(S_DIFF, zt)
            mlp(U_MLP2, B_MLP2, CH_MLP2)

        @block.scalar
        def _(act):
            def split_hi(u):
                if u.turn is None and u.base >= N_UNITS:
                    return
                act.wait_ge(w_landed[u.slot()], u_landed(u))
                if u.turn is not None or u.base >= RING:
                    act.wait_ge(w_used, u.value(1, 1 - RING))
                act.activation(hi_w[:, u.slot(), :], w_raw[:, u.slot(), :], ACT.Copy).then_inc(w_hi, 1)

            def u_landed(u):
                v = 32 * (u.base // RING + 1)
                return v if u.turn is None else u.turn * (32 * u.per // RING) + v

            def chunk_his(first, n, off, dst, dst0, scale=None):
                for k in range(n):
                    act.wait_ge(chunksT, first + (k | 1) + 1)
                    src = ps[:, off(k):off(k) + SEQ]
                    act.activation(dst[:, dst0 + k, :], src, ACT.Copy,
                                   scale=1.0 if scale is None else scale[:, k:k + 1]).then_inc(ch_act, 1)

            def chunk_affine(s, j):
                first = CH_AFTER[s]
                for k in range(KD):
                    act.wait_ge(chunksT, first + (k | 1) + 1)
                    if k >= 2:
                        act.wait_ge(ch_lo, first + k - 1)
                    off = chunk_off(s, k)
                    act.activation(affine[k % 2], ps[:, off:off + SEQ], ACT.Identity, scale=aff_a[:, j, k:k + 1],
                                   bias=aff_b[:, j, k:k + 1]).then_inc(ch_act, 1)

            def normalise_tile0(n):
                act.wait_ge(shift_done, n + 1)
                act.activation(zt[:, 0, :], zt[:, 0, :], ACT.Identity, scale=rstd[:, 0:1], bias=shift[:, :])\
                   .then_inc(norm_done[0], 1)

            def out_squares(s, base):
                for t in range(NT):
                    if t == 0:
                        act.wait_ge(tile0_done, s + 1)
                    else:
                        act.wait_ge(w_used, LAST_UNIT[s] + 1)
                    act.activation(zt[:, t, :], bank(base + 2 * t, 2), ACT.Square,
                                   accum_out=sq[:, t:t + 1]).then_inc(sq_done, 1)

            def x_squares(s, n):
                for t in range(NT):
                    if s >= 0:
                        act.wait_ge(norm_done[t], s + 1)
                    act.activation(zt[:, t, :], x[:, t, :], ACT.Square,
                                   accum_out=sq_x[:, t:t + 1]).then_inc(xsq_done, 1)

            def small_vectors():
                act.wait_ge(small_in, 2)
                act.activation(dk[:, 1, :], dk[:, 0, :], ACT.Exp, scale=-1.0).then_inc(small_exp, 1)
                act.activation(lam[:, 2:4], lam[:, 0:2], ACT.Exp).then_inc(small_exp, 1)

            def swiglu(u0, b0, n, between=None):
                def activation(b, i):
                    act.wait_ge(w_used, unit_of(b, i))
                    if b.turn is not None or i >= 1:
                        act.wait_ge(hid_done, b.value())
                    for t in range(NT):
                        pair = 4 + 2 * (i % 2)
                        ins = act.activation(act_s[:, t, 0:FF_B], ps[:, (pair + t) * BANK:(pair + t) * BANK + FF_B],
                                             ACT.Silu, scale=rstd_x[:, t:t + 1])
                    ins.then_inc(act_done, 1)

                def unit_of(b, i):
                    per_b = 3
                    if b.turn is None:
                        return u0 + 2 if i == 0 else u0 + 4 + per_b * (i - 1)
                    return b.turn * (per_b * b.per) + u0 + 4 + per_b * (i - 1)

                def hidden_hi(b, i):
                    act.wait_ge(hidT, b.value(1, 1))
                    off = (4 + 2 * (i % 2)) * BANK
                    act.activation(hT_hi[:, 0:2, :], ps[:, off:off + 2 * SEQ].rearrange("p (c n) -> p c n", c=2),
                                   ACT.Copy).then_inc(hidT_hi, 1)

                def step(u, b, i):
                    split_hi(u + AHEAD)
                    hidden_hi(b, i)
                    split_hi(u + (AHEAD + 1))
                    activation(b + 1, i + 1)
                    split_hi(u + (AHEAD + 2))

                split_hi(Count(u0 + AHEAD))
                act.wait_ge(rstd_x_done, n)
                split_hi(Count(u0 + AHEAD + 1))
                activation(Count(b0), 0)
                for i in range(2):
                    step(Count(u0 + 2 + 3 * i), Count(b0 + i), i)
                if between is not None:
                    between()
                with act.Fori(0, (N_FF - 3) // LOOP_STEPS) as turn:
                    for j in range(LOOP_STEPS):
                        step(Count(u0 + 8 + 3 * j, 3 * LOOP_STEPS, turn), Count(b0 + 2 + j, LOOP_STEPS, turn), 2 + j)
                hidden_hi(Count(b0 + N_FF - 1), N_FF - 1)
                split_hi(Count(u0 + 3 * N_FF - 1 + AHEAD))

            def mlp(u0, b0):
                def units(b, i, plus):
                    v = u0 + plus + 4 * i
                    return v if b.turn is None else b.turn * (4 * b.per) + v

                def activation(b, i):
                    act.wait_ge(w_used, units(b, i, 2 if i == 0 else 0))
                    if b.turn is not None or i >= 1:
                        act.wait_ge(hid_done, b.value())
                    pair = 4 + 2 * (i % 2)
                    act.activation(act_s, bank(pair, 2).rearrange("p (t n) -> p t n", t=NT), ACT.Relu)\
                       .then_inc(act_done, 1)

                def hidden_hi(b, i):
                    act.wait_ge(hidT, b.value(1, 1))
                    pair = 4 + 2 * (i % 2)
                    act.activation(hT_hi[:, :, :], bank(pair, 2).rearrange("p (c n) -> p c n", c=4),
                                   ACT.Copy).then_inc(hidT_hi, 1)

                def step(u, b, i):
                    split_hi(u + AHEAD)
                    hidden_hi(b, i)
                    split_hi(u + (AHEAD + 1))
                    activation(b + 1, i + 1)
                    split_hi(u + (AHEAD + 2))
                    split_hi(u + (AHEAD + 3))

                for half in range(2):
                    split_hi(Count(u0 + AHEAD + half))
                activation(Count(b0), 0)
                step(Count(u0 + 2), Count(b0), 0)
                with act.Fori(0, (N_MLP - 4) // 2) as turn:
                    for j in range(2):
                        step(Count(u0 + 6 + 4 * j, 8, turn), Count(b0 + 1 + j, 2, turn), 1 + j)
                for i in range(N_MLP - 3, N_MLP - 1):
                    step(Count(u0 + 2 + 4 * i), Count(b0 + i), i)
                hidden_hi(Count(b0 + N_MLP - 1), N_MLP - 1)
                for half in range(2):
                    split_hi(Count(u0 + 4 * N_MLP - 2 + AHEAD + half))

            def vector(dst, src):
                act.dma_start(dst, src).then_inc(ld_vec, 16)

            for col, name in ((C_F1, "ffn1_pre_norm"), (C_MIX, "mix_pre_norm"), (C_F2, "ffn2_pre_norm"), (C_C, "c_2")):
                vector(vec_rows[col:col + KD, :], d[name].rearrange("o (k p) -> (o k) p", p=P))
            split_hi(Count(0))
            act.wait_ge(vec_out, 1)
            chunk_his(CH_START, KD, lambda k: chunk_off(-1, k), xT_hi, 0, vec_cols[:, C_F1:C_F1 + KD])
            for u in range(1, AHEAD):
                split_hi(Count(u))
            x_squares(-1, 1)
            act.activation(c_act[:, :], vec_cols[:, C_C:C_C + KD], ACT.Silu).then_inc(c_done, 1)
            swiglu(U_FFN1, B_FFN1, 1, small_vectors)
            out_squares(S_FFN1, 0)

            chunk_his(CH_MIX, KD, lambda k: chunk_off(S_FFN1, k), xT_hi, 0, vec_cols[:, C_MIX:C_MIX + KD])
            x_squares(S_FFN1, 2)

            def mix_out(b):
                name, j = MIX_BLOCKS[b]
                act.wait_ge(w_used, U_MIX + 2 * b + 2)
                if b == 0:
                    act.wait_ge(rstd_x_done, 2)
                if b in (2, 3):
                    act.wait_ge(headT, b - 1)
                if name == "rg" and j == 0:
                    act.wait_ge(ret_s, RET_H)
                if name == "gr":
                    act.wait_ge(gated, 2)
                if name == "gn":
                    act.wait_ge(ret_y, RET_H)
                func = {"rg": ACT.Silu, "gr": ACT.Sigmoid, "gn": ACT.Sigmoid}.get(name, ACT.Copy)
                col = slice(j * BANK, (j + 1) * BANK)
                for t in range(NT):
                    dst = {"rq": stage[0][:, t, :], "rk": stage[1][:, t, :], "nq": stage[0][:, t, :],
                           "nk": stage[1][:, t, :], "rv": v_nat[:, t, col], "nv": nv[:, t, :],
                           "rg": silu_rg[j][:, t, :], "gr": g_ret[:, t, col], "gn": g_na[:, t, col]}[name]
                    ins = act.activation(dst, bank(4 + 2 * (b % 2) + t), func, scale=rstd_x[:, t:t + 1])
                ins.then_inc(proj_out, 1)

            u = U_MIX
            for slot in range(2 * N_MIX):
                if slot % 2 == 0 and slot >= 2:
                    mix_out(slot // 2 - 1)
                if 0 <= slot - 16 < NA_H:
                    h = slot - 16
                    act.wait_ge(at_t, h + 1)
                    if h >= 2:
                        act.wait_ge(at_o, h - 1)
                    act.activation(na_probsT[h % 2], bank(2), ACT.Copy).then_inc(at_p, 1)
                if 0 <= slot - 11 < RET_H:
                    h = slot - 11
                    act.wait_ge(ret_y, h + 1)
                    act.wait_ge(ret_sq, h)
                    if h >= 2:
                        act.wait_ge(ret_out, h - 1)
                    for t in range(NT):
                        off = (2 + h % 2) * BANK + t * RET_DV
                        ins = act.activation(squares_of[:, t, :], ps[:, off:off + RET_DV], ACT.Square,
                                             accum_out=head_sq[:, h % 2, t:t + 1])
                    ins.then_inc(ret_sq, 1)
                if slot in (5, 6, 10, 11):
                    h = (5, 6, 10, 11).index(slot)
                    act.wait_ge(exponent_done, h + 1)
                    act.activation(decays[h % 2], decays[h % 2], ACT.Exp).then_inc(decay_done, 1)
                if 0 <= slot - 15 < NA_H:
                    h = slot - 15
                    act.wait_ge(at_m, h + 1)
                    if h >= 2:
                        act.wait_ge(at_t, h - 1)
                        act.wait_ge(at_out, h - 1)
                    for t in range(NT):
                        ins = act.activation(na_probs[h % 2][:, t * SEQ:(t + 1) * SEQ], na_scores[:, t * SEQ:(t + 1) * SEQ],
                                             ACT.Exp, bias=top[:, 0, t:t + 1], accum_out=total[:, h % 2, t:t + 1])
                    ins.then_inc(at_e, 1)
                if slot == 25:
                    chunk_his(CH_NA, 4, lambda k: 6 * BANK + k * SEQ, hT_hi, 0)
                split_hi(Count(u + slot + AHEAD))
            mix_out(N_MIX - 1)
            chunk_his(CH_RET, KD, lambda k: k * SEQ, xT_hi, 0)
            for slot in range(2 * N_MIX, 2 * N_MIX + 5):
                split_hi(Count(u + slot + AHEAD))
            chunk_his(CH_MERGED, 4, lambda k: 6 * BANK + k * SEQ, hT_hi, 0)
            for slot in range(2 * N_MIX + 5, 2 * N_MIX + 8):
                split_hi(Count(u + slot + AHEAD))
            chunk_his(CH_MERGED + 4, 4, lambda k: k * SEQ, xT_hi, 4)
            for slot in range(2 * N_MIX + 8, 2 * N_MIX + 10):
                split_hi(Count(u + slot + AHEAD))
            out_squares(S_MIX, 4)
            chunk_his(CH_FFN2, KD, lambda k: chunk_off(S_MIX, k), xT_hi, 0, vec_cols[:, C_F2:C_F2 + KD])
            x_squares(S_MIX, 3)
            swiglu(U_FFN2, B_FFN2, 3)
            out_squares(S_FFN2, 0)
            act.wait_ge(mod_T, 1)
            act.activation(mod_rows[:, :], ps[0:96, 4 * BANK:4 * BANK + P], ACT.Copy).then_inc(mod_row, 1)
            chunk_affine(S_FFN2, 0)

            def attention(u0, pb, hb, ab, ch_o, diff):
                def project_out(b):
                    name, j = QKV_BLOCKS[b]
                    n = 2 * j + (name == "k")
                    act.wait_ge(w_used, u0 + 2 * b + 2)
                    if name != "v" and j == 1:
                        act.wait_ge(headT, hb + n - 1)
                    for t in range(NT):
                        dst = v2[:, t, j * BANK:(j + 1) * BANK] if name == "v" else stage2[n % 2][:, t, :]
                        ins = act.activation(dst, bank(4 + 2 * (b % 2) + t), ACT.Copy)
                    ins.then_inc(proj_out, 1)

                def weights_out(c):
                    act.wait_ge(at_t, ab + c + 1)
                    act.wait_ge(at_o, ab + c)
                    n = 3 * P if diff else 6 * P
                    act.activation(probsT[:, 0:n], ps[:, 2 * BANK:2 * BANK + n], ACT.Copy).then_inc(at_p, 1)

                def exps(c):
                    act.wait_ge(at_m, ab + c + 1)
                    if diff:
                        act.wait_ge(at_w, c)
                    elif c >= 2:
                        act.wait_ge(at_out, ab + c - 1)
                    for e in range(2):
                        for t in range(NT):
                            pr = probs[:, e * 3 * P:e * 3 * P + P] if t == 0 else probs[:, e * 3 * P + P:(e + 1) * 3 * P]
                            ins = act.activation(pr, pr, ACT.Exp, bias=top[:, e, t:t + 1],
                                                 accum_out=total[:, c % 2, 2 * e + t:2 * e + t + 1])
                    ins.then_inc(at_e, 1)

                def squares(c):
                    act.wait_ge(at_o, ab + c + 1)
                    act.wait_ge(at_sq, c)
                    act.wait_ge(at_out, ab + c)
                    for t in range(NT):
                        off = 3 * BANK + SEQ + t * P
                        ins = act.activation(squares_of[:, t, 0:P], ps[:, off:off + P], ACT.Square,
                                             accum_out=head_sq[:, c % 4, t:t + 1])
                    ins.then_inc(at_sq, 1)

                before = []
                for slot, between, events in ATTENTION:
                    for event in before:
                        if event[0] == "T":
                            half = int(event[1:])
                            base = 4 * BANK if half == 0 else 0
                            chunk_his(ch_o + 4 * half, 4, lambda k: base + k * SEQ, xT_hi, 4 * half)
                    if slot is not None and 2 <= slot <= 12 and slot % 2 == 0:
                        project_out(slot // 2 - 1)
                    for event in before:
                        if event[0] == "W":
                            weights_out(int(event[1:]))
                    for event in before:
                        if event[0] == "O" and diff:
                            squares(int(event[1:]))
                    for event in before:
                        if event[0] == "S":
                            exps(int(event[1:]))
                    if slot is not None:
                        split_hi(Count(u0 + slot + AHEAD))
                    before = events

            attention(U_MOBA, PB_MOBA, 4, NA_H, CH_MOBA_O, False)
            normalise_tile0(0)
            chunk_affine(S_MOBA, 1)
            mlp(U_MLP1, B_MLP1)
            normalise_tile0(1)
            chunk_affine(S_MLP1, 2)
            attention(U_DIFF, PB_DIFF, 8, NA_H + 8, CH_DIFF_O, True)
            normalise_tile0(2)
            chunk_affine(S_DIFF, 3)
            mlp(U_MLP2, B_MLP2)

        @block.vector
        def _(vec):
            steps = Steps(vec_step)

            def then(ins):
                steps.inc(ins)
                steps.wait(vec)

            def split_lo(u):
                if u.turn is None and u.base >= N_UNITS:
                    return
                vec.wait_ge(w_hi, u.value(1, 1))
                vec.tensor_tensor(lo_w[:, u.slot(), :], w_raw[:, u.slot(), :], hi_w[:, u.slot(), :].bitcast(F32),
                                  ALU.subtract).then_inc(w_lo, 1)

            def chunk_los(first, n, off, hi, lo, dst0, scale=None):
                for k in range(n):
                    vec.wait_ge(ch_act, first + (k | 1) + 1)
                    src = ps[:, off(k):off(k) + SEQ]
                    h = hi[:, dst0 + k, :].bitcast(F32)
                    if scale is None:
                        ins = vec.tensor_tensor(lo[:, dst0 + k, :], src, h, ALU.subtract)
                    else:
                        ins = vec.scalar_tensor_tensor(out=lo[:, dst0 + k, :], in0=src, scalar=scale[:, k:k + 1],
                                                       in1=h, op0=ALU.mult, op1=ALU.subtract)
                    ins.then_inc(ch_lo, 1)

            def chunk_splits(s):
                first = CH_AFTER[s]
                for k in range(KD):
                    vec.wait_ge(ch_act, first + k + 1)
                    then(vec.tensor_copy(xT_hi[:, k, :], affine[k % 2]))
                    vec.tensor_tensor(xT_lo[:, k, :], affine[k % 2], xT_hi[:, k, :].bitcast(F32), ALU.subtract)\
                       .then_inc(ch_lo, 1)

            def rsqrt(dst, src, n, scale, eps):
                v, i, y, h = (newton[:, j, 0:n] for j in range(4))
                k = 3.0 / 8.0
                then(vec.tensor_scalar(v, src, scale / k ** 2, eps / k ** 2, ALU.mult, ALU.add))
                then(vec.tensor_scalar(i.bitcast(U32), v.bitcast(U32), 1, None, ALU.logical_shift_right))
                then(vec.tensor_scalar(y.bitcast(I32), i.bitcast(I32), -1.0, float(0x5F3759DF), ALU.mult, ALU.add))
                then(vec.tensor_tensor(h, y, y, ALU.mult))
                then(vec.tensor_tensor(h, h, v, ALU.mult))
                then(vec.scalar_tensor_tensor(out=h, in0=h, scalar=-10.0 / 3.0, in1=h, op0=ALU.add, op1=ALU.mult))
                then(vec.scalar_tensor_tensor(out=y, in0=h, scalar=5.0, in1=y, op0=ALU.add, op1=ALU.mult))
                then(vec.tensor_tensor(h, y, y, ALU.mult))
                then(vec.scalar_tensor_tensor(out=h, in0=h, scalar=-0.5 * k ** 2, in1=v, op0=ALU.mult, op1=ALU.mult))
                then(vec.scalar_tensor_tensor(out=dst, in0=h, scalar=1.5, in1=y, op0=ALU.add, op1=ALU.mult))

            def x_factor(n):
                vec.wait_ge(xsq_done, NT * n)
                rsqrt(rstd_x[:, :], sq_x[:, :], NT, 1.0 / D, RMS_EPS)
                vec.engine_nop().then_inc(rstd_x_done, 1)

            def rms_update(s, n, base, row, weight):
                vec.wait_ge(sq_done, NT * (n + 1))
                rsqrt(rstd[:, :], sq[:, :], NT, 1.0 / D, RMS_EPS)
                vec.wait_ge(ld_row, 16 * (n + 1))
                for t in range(NT):
                    then(vec.scalar_tensor_tensor(out=zt[:, t, :], in0=bank(base + 2 * t, 2), scalar=rstd[:, t:t + 1],
                                                  in1=row, op0=ALU.mult, op1=ALU.mult))
                    vec.scalar_tensor_tensor(out=x[:, t, :], in0=zt[:, t, :], scalar=weight, in1=x[:, t, :],
                                             op0=ALU.mult, op1=ALU.add).then_inc(norm_done[t], 1)

            def layer_norm(s, n, base):
                for t in range(NT):
                    if t == 0:
                        vec.wait_ge(tile0_done, s + 1)
                        vec.wait_ge(ld_row, 16 * 3 * (n + 2))
                    else:
                        vec.wait_ge(w_used, LAST_UNIT[s] + 1)
                    if n >= 1:
                        vec.wait_ge(x_new, NT * (n - 1) + t + 1)
                    z = zt[:, t, :]
                    then(vec.tensor_tensor(z, bank(base + 2 * t, 2), row_a, ALU.mult))
                    then(vec.scalar_tensor_tensor(out=z, in0=x[:, t, :], scalar=ALPHA, in1=z, op0=ALU.mult, op1=ALU.add))
                    for c in range(2):
                        ins = vec.bn_stats(bst[:, t, c, :], zt[:, t, c * BANK:(c + 1) * BANK])
                    then(ins)
                    then(vec.bn_aggr(moments[:, t, :], bst[:, t, :, :].rearrange("p c n -> p (c n)")))
                rsqrt(rstd[:, :], moments[:, :, 1], NT, 1.0, LN_EPS)
                if s != S_MLP2:
                    vec.scalar_tensor_tensor(out=shift[:, :], in0=moments[:, 0, 0:1], scalar=-1.0, in1=rstd[:, 0:1],
                                             op0=ALU.mult, op1=ALU.mult).then_inc(shift_done, 1)
                    vec.tensor_scalar(zt[:, 1, :], zt[:, 1, :], moments[:, 1, 0:1], rstd[:, 1:2], ALU.subtract,
                                      ALU.mult).then_inc(norm_done[1], 1)
                    return
                for t in range(NT):
                    z = zt[:, t, :]
                    then(vec.scalar_tensor_tensor(out=z, in0=z, scalar=moments[:, t, 0:1], in1=row_g,
                                                  op0=ALU.subtract, op1=ALU.mult))
                    vec.scalar_tensor_tensor(out=x[:, t, :], in0=z, scalar=rstd[:, t:t + 1], in1=row_b,
                                             op0=ALU.mult, op1=ALU.add).then_inc(x_fin, 1)

            def hidden_lo(b, i, chunks):
                vec.wait_ge(hidT_hi, b.value(1, 1))
                src = ps[:, (4 + 2 * (i % 2)) * BANK:(4 + 2 * (i % 2)) * BANK + chunks * SEQ]
                vec.tensor_tensor(hT_lo[:, 0:chunks, :], src.rearrange("p (c n) -> p c n", c=chunks),
                                  hT_hi[:, 0:chunks, :].bitcast(F32), ALU.subtract).then_inc(hidT_lo, 1)

            def piece_half(p, half):
                vec.wait_ge(mod_landed[half], p.value(16, 16))
                if p.turn is not None or p.base >= 2:
                    if half == 0:
                        vec.wait_ge(piece_cols, p.value(1, -1))
                acc = piece_acc[:, p.slot(2), :]
                for k in range(4):
                    c = 4 * half + k
                    row = aux[:, half * UNIT + k * BANK:half * UNIT + (k + 1) * BANK]
                    if c == 0:
                        ins = vec.tensor_scalar(acc, row, c_act[:, 0:1], None, ALU.mult)
                    else:
                        vec.wait_ge(mod_step, p.value(KD, c))
                        ins = vec.scalar_tensor_tensor(out=acc, in0=row, scalar=c_act[:, c:c + 1], in1=acc,
                                                       op0=ALU.mult, op1=ALU.add)
                    ins.then_inc(mod_step, 1)

            def piece_result(p, i, col):
                vec.wait_ge(piece_cols, p.value(1, 1))
                off = (5 + 2 * (i % 2)) * BANK + col
                vec.tensor_tensor(mod_cols[:, bass.ds(p.value(4), 4)], ps[:, off:off + 4],
                                  adab_cols[:, bass.ds(p.value(4), 4)], ALU.add).then_inc(piece_out, 1)

            def swiglu(u0, b0, p0, between=None):
                def product(b, i):
                    vec.wait_ge(act_done, b.value(1, 1))
                    if b.turn is not None or i >= 1:
                        vec.wait_ge(hidT, b.value())
                    for t in range(NT):
                        off = (4 + 2 * (i % 2) + t) * BANK + FF_B
                        ins = vec.scalar_tensor_tensor(out=hid[:, t, 0:FF_B], in0=ps[:, off:off + FF_B],
                                                       scalar=rstd_x[:, t:t + 1], in1=act_s[:, t, 0:FF_B],
                                                       op0=ALU.mult, op1=ALU.mult)
                    ins.then_inc(hid_done, 1)

                def step(u, b, i):
                    piece = b + (p0 - b0)
                    split_lo(u + AHEAD)
                    piece_half(piece + 1, 0)
                    hidden_lo(b, i, 2)
                    piece_result(piece, i, 0)
                    piece_half(piece + 1, 1)
                    split_lo(u + (AHEAD + 1))
                    product(b + 1, i + 1)
                    split_lo(u + (AHEAD + 2))

                split_lo(Count(u0 + AHEAD))
                piece_half(Count(p0), 0)
                split_lo(Count(u0 + AHEAD + 1))
                product(Count(b0), 0)
                piece_half(Count(p0), 1)
                for i in range(2):
                    step(Count(u0 + 2 + 3 * i), Count(b0 + i), i)
                if between is not None:
                    between()
                with vec.Fori(0, (N_FF - 3) // LOOP_STEPS) as turn:
                    for j in range(LOOP_STEPS):
                        step(Count(u0 + 8 + 3 * j, 3 * LOOP_STEPS, turn), Count(b0 + 2 + j, LOOP_STEPS, turn), 2 + j)
                hidden_lo(Count(b0 + N_FF - 1), N_FF - 1, 2)
                piece_result(Count(p0 + N_FF - 1), N_FF - 1, 0)
                for half in range(2):
                    piece_half(Count(p0 + N_FF), half)
                piece_result(Count(p0 + N_FF), N_FF - 1, 4)

            def mlp(u0, b0):
                def product(b, i):
                    vec.wait_ge(act_done, b.value(1, 1))
                    if b.turn is not None or i >= 1:
                        vec.wait_ge(hidT, b.value())
                    vec.tensor_tensor(hid, act_s, act_s, ALU.mult).then_inc(hid_done, 1)

                def step(u, b, i):
                    split_lo(u + AHEAD)
                    hidden_lo(b, i, 4)
                    split_lo(u + (AHEAD + 1))
                    product(b + 1, i + 1)
                    split_lo(u + (AHEAD + 2))
                    split_lo(u + (AHEAD + 3))

                for half in range(2):
                    split_lo(Count(u0 + AHEAD + half))
                product(Count(b0), 0)
                step(Count(u0 + 2), Count(b0), 0)
                with vec.Fori(0, (N_MLP - 4) // 2) as turn:
                    for j in range(2):
                        step(Count(u0 + 6 + 4 * j, 8, turn), Count(b0 + 1 + j, 2, turn), 1 + j)
                for i in range(N_MLP - 3, N_MLP - 1):
                    step(Count(u0 + 2 + 4 * i), Count(b0 + i), i)
                hidden_lo(Count(b0 + N_MLP - 1), N_MLP - 1, 4)
                split_lo(Count(u0 + 4 * N_MLP - 2 + AHEAD))

            def small_vectors():
                vec.wait_ge(ld_const, CONST_LOADS)
                then(vec.tensor_scalar(dk[:, 5, :], decay[:, :], -1.0, None, ALU.mult))
                vec.tensor_tensor(dk[:, 0, :], decay[:, :], dk[:, 5, :], ALU.max).then_inc(small_in, 1)
                for i in range(2):
                    then(vec.tensor_tensor(lam_prod[:, :], lam_in[:, 2 * i, :], lam_in[:, 2 * i + 1, :], ALU.mult))
                    ins = vec.tensor_reduce(lam[:, i:i + 1], lam_prod[:, :], AX.X, ALU.add)
                    if i == 0:
                        then(ins)
                ins.then_inc(small_in, 1)
                vec.wait_ge(small_exp, 2)
                z, s, w, acc, tmp = dk[:, 1, :], dk[:, 2, :], dk[:, 3, :], dk[:, 4, :], dk[:, 5, :]
                then(vec.tensor_scalar(tmp, z, 2.0, None, ALU.add))
                then(vec.reciprocal(tmp, tmp))
                then(vec.tensor_tensor(s, z, tmp, ALU.mult))
                then(vec.tensor_tensor(w, s, s, ALU.mult))
                then(vec.tensor_scalar(acc, w, 1.0 / 17, None, ALU.mult))
                for odd in (15, 13, 11, 9, 7, 5, 3):
                    then(vec.scalar_tensor_tensor(out=acc, in0=acc, scalar=1.0 / odd, in1=w, op0=ALU.add, op1=ALU.mult))
                then(vec.scalar_tensor_tensor(out=acc, in0=acc, scalar=1.0, in1=s, op0=ALU.add, op1=ALU.mult))
                then(vec.tensor_scalar(tmp, decay[:, :], 0.0, None, ALU.min))
                then(vec.scalar_tensor_tensor(out=decay[:, :], in0=acc, scalar=-2.0, in1=tmp, op0=ALU.mult, op1=ALU.add))
                then(vec.tensor_tensor(lam[:, 0:1], lam[:, 3:4], lam[:, 2:3], ALU.subtract))
                then(vec.tensor_scalar(lam[:, 0:1], lam[:, 0:1], -LAMBDA_INIT, None, ALU.add))
                then(vec.tensor_scalar(subln[:, :], subln[:, :], 1.0 - LAMBDA_INIT, None, ALU.mult))

            split_lo(Count(0))
            vec.wait_ge(vecT, 1)
            then(vec.tensor_copy(vec_cols[:, :], ps[:, 6 * BANK:6 * BANK + 96]))
            vec.tensor_copy(adab_cols[:, :], ps[:, 7 * BANK:7 * BANK + 96]).then_inc(vec_out, 1)
            chunk_los(CH_START, KD, lambda k: chunk_off(-1, k), xT_hi, xT_lo, 0, vec_cols[:, C_F1:C_F1 + KD])
            for u in range(1, AHEAD):
                split_lo(Count(u))
            x_factor(1)
            vec.wait_ge(c_done, 1)
            swiglu(U_FFN1, B_FFN1, 0, small_vectors)
            rms_update(S_FFN1, 0, 0, row_ffn, 0.5)

            chunk_los(CH_MIX, KD, lambda k: chunk_off(S_FFN1, k), xT_hi, xT_lo, 0, vec_cols[:, C_MIX:C_MIX + KD])
            split_lo(Count(U_MIX + AHEAD - 1))
            x_factor(2)
            vec.wait_ge(ld_tab, 16 * 3)
            for slot in range(2 * N_MIX):
                if 0 <= slot - 15 < NA_H:
                    h = slot - 15
                    vec.wait_ge(at_s, h + 1)
                    vec.wait_ge(bias_done, h + 1)
                    if h == 0:
                        vec.wait_ge(ret_y, RET_H)
                    else:
                        vec.wait_ge(at_e, h)
                    then(vec.scalar_tensor_tensor(out=na_scores, in0=bank(h % 2), scalar=NA_D ** -0.5,
                                                  in1=bias[h % 2].rearrange("p t n -> p (t n)"),
                                                  op0=ALU.mult, op1=ALU.add))
                    then(vec.tensor_reduce(top[:, 1, :], na_scores.rearrange("p (t n) -> p t n", t=NT), AX.X, ALU.max))
                    vec.tensor_scalar(top[:, 0, :], top[:, 1, :], -1.0, None, ALU.mult).then_inc(at_m, 1)
                if slot in (2, 4):
                    n = slot // 2 - 1
                    vec.wait_ge(proj_out, PB_MIX + n + 1)
                    if n == 1:
                        vec.wait_ge(rot_done, 1)
                    for t in range(NT):
                        rows = stage[n][:, t, :].rearrange("p (h c n) -> p h c n", h=RET_H, c=2)
                        a, b = rows[:, :, 0, :], rows[:, :, 1, :]
                        cos, sin = (rot1[:, i, t, :].unsqueeze(1).broadcast_to([P, RET_H, 64]) for i in range(2))
                        tm = [rope1_t[i].rearrange("p (h n) -> p h n", h=RET_H) for i in range(4)]
                        vec.tensor_tensor(tm[0], a, cos, ALU.mult)
                        vec.tensor_tensor(tm[1], b, sin, ALU.mult)
                        vec.tensor_tensor(tm[2], a, sin, ALU.mult)
                        then(vec.tensor_tensor(tm[3], b, cos, ALU.mult))
                        vec.tensor_tensor(a, tm[0], tm[1], ALU.subtract)
                        ins = vec.tensor_tensor(b, tm[2], tm[3], ALU.add)
                        if t == 0:
                            then(ins)
                    ins.then_inc(rot_done, 1)
                if slot in (4, 6, 8, 10):
                    n = slot // 2 - 2
                    vec.wait_ge(headT, n + 1)
                    vec.tensor_copy([qT, kT, nqT, nkT][n], bank(2 * (n % 2), 2).rearrange("p (c n) -> p c n", c=4))\
                       .then_inc(headT_out, 1)
                if 0 <= slot - 9 < RET_H:
                    h = slot - 9
                    vec.wait_ge(ret_s, h + 1)
                    vec.wait_ge(decay_done, h + 1)
                    if h >= 2:
                        vec.wait_ge(ret_y, h - 1)
                    vec.scalar_tensor_tensor(out=ret_probs[h % 2], in0=bank(h % 2), scalar=RET_DK ** -0.5,
                                             in1=decays[h % 2], op0=ALU.mult, op1=ALU.mult).then_inc(ret_p, 1)
                if slot in (5, 6, 10, 11):
                    h = (5, 6, 10, 11).index(slot)
                    if h >= 2:
                        vec.wait_ge(ret_p, h - 1)
                    then(vec.tensor_scalar(decay_tmp, relu_t[0], decay[:, h:h + 1], None, ALU.mult))
                    vec.scalar_tensor_tensor(out=decays[h % 2], in0=relu_t[1], scalar=decay[:, RET_H + h:RET_H + h + 1],
                                             in1=decay_tmp, op0=ALU.mult, op1=ALU.add).then_inc(exponent_done, 1)
                if 0 <= slot - 11 < RET_H:
                    h = slot - 11
                    vec.wait_ge(ret_sq, h + 1)
                    rsqrt(head_rstd[:, 0:NT], head_sq[:, h % 2, :], NT, 1.0 / RET_DV, RMS_EPS)
                    for t in range(NT):
                        off = (2 + h % 2) * BANK + t * RET_DV
                        ins = vec.tensor_scalar(y_nat[:, t, h * RET_DV:(h + 1) * RET_DV], ps[:, off:off + RET_DV],
                                                head_rstd[:, t:t + 1], None, ALU.mult)
                    ins.then_inc(ret_out, 1)
                if slot in (16, 18):
                    j = slot // 2 - 8
                    vec.wait_ge(proj_out, PB_MIX + 8 + j)
                    vec.wait_ge(ret_out, RET_H)
                    col = slice(j * BANK, (j + 1) * BANK)
                    vec.tensor_tensor(y_nat[:, :, col], y_nat[:, :, col], silu_rg[j], ALU.mult).then_inc(gated, 1)
                if 0 <= slot - 17 < NA_H:
                    h = slot - 17
                    vec.wait_ge(at_o, h + 1)
                    then(vec.reciprocal(inv[:, 0:NT], total[:, h % 2, 0:NT]))
                    src = ps[:, 3 * BANK:3 * BANK + NT * NA_D].rearrange("p (t n) -> p t n", t=NT)
                    vec.tensor_tensor(nao[:, :, h * NA_D:(h + 1) * NA_D], src,
                                      inv[:, 0:NT].unsqueeze(2).broadcast_to([P, NT, NA_D]), ALU.mult)\
                       .then_inc(at_out, 1)
                if slot == 25:
                    chunk_los(CH_NA, 4, lambda k: 6 * BANK + k * SEQ, hT_hi, hT_lo, 0)
                split_lo(Count(U_MIX + slot + AHEAD))

            def both(first):
                return bank(first, 2).rearrange("p (t n) -> p t n", t=NT)

            u = U_MIX + 2 * N_MIX
            cols = [slice(0, BANK), slice(BANK, 2 * BANK)]
            chunk_los(CH_RET, KD, lambda k: k * SEQ, xT_hi, xT_lo, 0)
            split_lo(Count(u + AHEAD))
            for n in range(2):
                vec.wait_ge(w_used, u + n + 1)
                vec.wait_ge(proj_out, PB_MIX + N_MIX)
                vec.tensor_tensor(g_na[:, :, cols[n]], g_na[:, :, cols[n]], both(6 - 2 * n), ALU.mult)\
                   .then_inc(half_merged, 1)
                split_lo(Count(u + n + 1 + AHEAD))
            split_lo(Count(u + 3 + AHEAD))

            def merge(n):
                vec.wait_ge(w_used, u + 4 + 2 * n)
                vec.wait_ge(half_merged, n + 1)
                then(vec.tensor_tensor(g_ret[:, :, cols[n]], g_ret[:, :, cols[n]], both(2 * n), ALU.mult))
                vec.tensor_tensor(g_ret[:, :, cols[n]], g_ret[:, :, cols[n]], g_na[:, :, cols[n]], ALU.add)\
                   .then_inc(merged, 1)

            merge(0)
            split_lo(Count(u + 4 + AHEAD))
            chunk_los(CH_MERGED, 4, lambda k: 6 * BANK + k * SEQ, hT_hi, hT_lo, 0)
            split_lo(Count(u + 5 + AHEAD))
            merge(1)
            split_lo(Count(u + 6 + AHEAD))
            split_lo(Count(u + 7 + AHEAD))
            chunk_los(CH_MERGED + 4, 4, lambda k: k * SEQ, xT_hi, xT_lo, 4)
            split_lo(Count(u + 8 + AHEAD))
            rms_update(S_MIX, 1, 4, row_a, 1.0)
            chunk_los(CH_FFN2, KD, lambda k: chunk_off(S_MIX, k), xT_hi, xT_lo, 0, vec_cols[:, C_F2:C_F2 + KD])
            split_lo(Count(U_FFN2 + AHEAD - 1))
            x_factor(3)
            swiglu(U_FFN2, B_FFN2, N_PIECE // 2)

            rms_update(S_FFN2, 2, 0, row_ffn, 0.5)

            vec.wait_ge(piece_out, N_PIECE)
            mods = mod_cols[:, :].rearrange("p (l g k) -> p l g k", l=2, g=6)
            for g in (1, 4):
                then(vec.tensor_scalar(mods[:, :, g:g + 2, :], mods[:, :, g:g + 2, :], 1.0, None, ALU.add))
            ln_g = vec_cols[:, C_LNG:C_LNG + 4 * KD].rearrange("p (j k) -> p j k", k=KD)
            ln_b = vec_cols[:, C_LNB:C_LNB + 4 * KD].rearrange("p (j k) -> p j k", k=KD)
            vec.tensor_copy(aff_a[:, 0, :], mods[:, 0, 1, :])
            then(vec.tensor_copy(aff_b[:, 0, :], mods[:, 0, 0, :]))
            for j in range(1, 4):
                layer, g = (0, 3) if j == 1 else (1, 3 * (j - 2))
                vec.tensor_tensor(aff_a[:, j, :], ln_g[:, j - 1, :], mods[:, layer, g + 1, :], ALU.mult)
                then(vec.tensor_tensor(aff_b[:, j, :], ln_b[:, j - 1, :], mods[:, layer, g + 1, :], ALU.mult))
                ins = vec.tensor_tensor(aff_b[:, j, :], aff_b[:, j, :], mods[:, layer, g, :], ALU.add)
            ins.then_inc(mod_fin, 1)
            chunk_splits(S_FFN2)
            split_lo(Count(U_MOBA + AHEAD - 1))

            def attention(u0, pb, hb, ab, ch_o, diff):
                def rotate(n):
                    buf = stage2[n % 2]
                    vec.wait_ge(proj_out, pb + 3 * (n // 2) + n % 2 + 1)
                    if n == 0:
                        vec.wait_ge(ld_tab, 16 * 5)
                    vec.wait_ge(rot_done, hb - 2 + n)
                    rows = buf.rearrange("p t (h n) -> p t h n", n=HD)
                    a, b = rows[:, :, :, 0:ROT], rows[:, :, :, ROT:2 * ROT]
                    cos, sin = (rot2[:, i, :, :].rearrange("p t (h n) -> p t h n", n=ROT) for i in range(2))
                    tm = [r.rearrange("p t (h n) -> p t h n", n=ROT) for r in rope2_t]
                    vec.tensor_tensor(tm[0], a, cos, ALU.mult)
                    vec.tensor_tensor(tm[1], b, sin, ALU.mult)
                    vec.tensor_tensor(tm[2], a, sin, ALU.mult)
                    then(vec.tensor_tensor(tm[3], b, cos, ALU.mult))
                    vec.tensor_tensor(a, tm[0], tm[1], ALU.subtract)
                    vec.tensor_tensor(b, tm[2], tm[3], ALU.add).then_inc(rot_done, 1)

                def heads_out(n):
                    vec.wait_ge(headT, hb + n + 1)
                    if diff and n == 1:
                        vec.wait_ge(x_new, 2 * NT)
                    dst = [q2T[0], k2T[0], q2T[1], k2T[1]][n]
                    vec.tensor_copy(dst, bank(0, 2).rearrange("p (c n) -> p c n", c=4)).then_inc(headT_out, 1)

                def scores(c):
                    vec.wait_ge(at_s, ab + c + 1)
                    vec.wait_ge(at_e, ab + c)
                    if diff:
                        vec.wait_ge(at_w, c)
                    else:
                        vec.wait_ge(at_t, ab + c)
                    src = bank(0, 2).rearrange("p (e n) -> p e n", e=2)[:, :, 0:3 * P]
                    dst = probs.rearrange("p (e n) -> p e n", e=2)
                    mask = causal[:, :].unsqueeze(1).broadcast_to([P, 2, 3 * P])
                    then(vec.scalar_tensor_tensor(out=dst, in0=src, scalar=HD ** -0.5, in1=mask, op0=ALU.mult,
                                                  op1=ALU.add))
                    vec.tensor_reduce(top[:, :, 0], dst[:, :, 0:P], AX.X, ALU.max)
                    then(vec.tensor_reduce(top[:, :, 1], dst[:, :, P:3 * P], AX.X, ALU.max))
                    vec.tensor_scalar(top[:, :, :], top[:, :, :], -1.0, None, ALU.mult).then_inc(at_m, 1)

                def combine(c):
                    vec.wait_ge(at_e, ab + c + 1)
                    vec.wait_ge(at_t, ab + c)
                    then(vec.reciprocal(inv[:, :], total[:, c % 2, :]))
                    then(vec.tensor_scalar(inv[:, 2:4], inv[:, 2:4], lam[:, 0:1], None, ALU.mult))
                    tiles = [slice(0, P), slice(P, 3 * P)]
                    for t in range(NT):
                        ins = vec.tensor_scalar(probs_w[:, tiles[t]], probs[:, tiles[t]], inv[:, t:t + 1], None, ALU.mult)
                    then(ins)
                    for t in range(NT):
                        second = probs[:, 3 * P:6 * P][:, tiles[t]]
                        ins = vec.scalar_tensor_tensor(out=probs_w[:, tiles[t]], in0=second, scalar=inv[:, 2 + t:3 + t],
                                                       in1=probs_w[:, tiles[t]], op0=ALU.mult, op1=ALU.add)
                    ins.then_inc(at_w, 1)

                def norms(c, n):
                    k = c % 4
                    rsqrt(head_rstd[:, 0:NT * n], head_sq[:, k:k + n, :].rearrange("p c t -> p (c t)"), NT * n, 1.0 / P,
                          SUBLN_EPS)
                    heads = o2[:, :, c * P:(c + n) * P].rearrange("p t (c n) -> p t c n", c=n)
                    factor = head_rstd[:, 0:NT * n].rearrange("p (c t) -> p t c", t=NT).unsqueeze(3)
                    return vec.tensor_tensor(heads, heads, factor.broadcast_to([P, NT, n, P]), ALU.mult)

                def outputs(c):
                    off = 3 * BANK + SEQ
                    if diff:
                        vec.wait_ge(at_sq, c + 1)
                        ins = vec.tensor_tensor(o2[:, :, c * P:(c + 1) * P],
                                                ps[:, off:off + NT * P].rearrange("p (t n) -> p t n", t=NT),
                                                subln[:, :].unsqueeze(1).broadcast_to([P, NT, P]), ALU.mult)
                        if c % 4 == 3:
                            then(ins)
                            ins = norms(c, 1)
                    else:
                        vec.wait_ge(at_o, ab + c + 1)
                        if c % 4 < 3:
                            vec.wait_ge(at_p, ab + c + 2)
                        then(vec.reciprocal(inv[:, :], total[:, c % 2, :]))
                        factor = inv[:, :].rearrange("p (e t) -> p e t", e=2).unsqueeze(3).broadcast_to([P, 2, NT, HD])
                        ins = vec.tensor_tensor(
                            o2[:, :, c * P:(c + 1) * P].rearrange("p t (e n) -> p e t n", e=2),
                            ps[:, off:off + 4 * HD].rearrange("p (e t n) -> p e t n", e=2, t=NT), factor, ALU.mult)
                    ins.then_inc(at_out, 1)

                before = []
                for slot, between, events in ATTENTION:
                    for event in before:
                        if event[0] == "T":
                            n = int(event[1:])
                            base = 4 * BANK if n == 0 else 0
                            chunk_los(ch_o + 4 * n, 4, lambda k: base + k * SEQ, xT_hi, xT_lo, 4 * n)
                    for event in before:
                        if event[0] == "S":
                            scores(int(event[1:]))
                    for event in before:
                        n = int(event[1:])
                        if event[0] == "O":
                            outputs(n)
                        if event[0] == "H":
                            heads_out(n)
                    if slot in (2, 4, 8, 10):
                        rotate((2, 4, 8, 10).index(slot))
                    for event in between:
                        heads_out(int(event[1:]))
                    for event in before:
                        if event[0] == "S" and diff:
                            combine(int(event[1:]))
                    if diff and ("O2" in before or "O6" in before):
                        c = 2 if "O2" in before else 6
                        vec.wait_ge(at_out, ab + c + 1)
                        then(norms(c - 2, 3))
                    if slot is not None and slot < 15:
                        split_lo(Count(u0 + slot + AHEAD))
                    before = events

            attention(U_MOBA, PB_MOBA, 4, NA_H, CH_MOBA_O, False)
            layer_norm(S_MOBA, 0, 4)
            chunk_splits(S_MOBA)
            split_lo(Count(U_MLP1 + AHEAD - 1))
            mlp(U_MLP1, B_MLP1)
            layer_norm(S_MLP1, 1, 0)
            chunk_splits(S_MLP1)
            split_lo(Count(U_DIFF + AHEAD - 1))
            attention(U_DIFF, PB_DIFF, 8, NA_H + 8, CH_DIFF_O, True)
            layer_norm(S_DIFF, 2, 4)
            chunk_splits(S_DIFF)
            split_lo(Count(U_MLP2 + AHEAD - 1))
            mlp(U_MLP2, B_MLP2)
            layer_norm(S_MLP2, 3, 0)

        @block.gpsimd
        def _(pool):
            def vector(dst, src):
                pool.dma_start(dst, src).then_inc(ld_vec2, 16)

            vector(vec_rows[C_LNG:C_LNG + 4 * KD, :], d["ln_g_2"].rearrange("l j (k p) -> (l j k) p", p=P))
            vector(vec_rows[C_LNB:C_LNB + 4 * KD, :], d["ln_b_2"].rearrange("l j (k p) -> (l j k) p", p=P))
            vector(adab_rows[:, :], d["ada_b_2"].rearrange("l (k p) -> (l k) p", p=P))
            pool.memset(ones[:, :], 1.0).then_inc(ones_set, 1)
            pool.memset(rel[:, :], 0.0).then_inc(rel_zero, 1)

            def const(dst, src):
                pool.dma_start(dst, src).then_inc(ld_const, 16)

            const(decay[:, 0:RET_H], d["ret_decay_fwd"].to_broadcast([P, RET_H]))
            const(decay[:, RET_H:2 * RET_H], d["ret_decay_bwd"].to_broadcast([P, RET_H]))
            for i, name in enumerate(("diff_lam_q1_2", "diff_lam_k1_2", "diff_lam_q2_2", "diff_lam_k2_2")):
                const(lam_in[:, i, :], d[name].to_broadcast([P, HD]))
            const(subln[:, :], d["diff_subln_g_2"].to_broadcast([P, P]))
            const(na_mask[:, :], d["na_mask"])

            def row(dst, src):
                pool.dma_start(dst, src.to_broadcast([P, D])).then_inc(ld_row, 16)

            def modulation(layer):
                w = d["ada_w_2"][layer].rearrange("(k p) n -> p k n", p=P)
                p0 = layer * (N_PIECE // 2)

                def piece(p, i):
                    for half in range(2):
                        if p.turn is not None or p.base >= 1:
                            pool.wait_ge(mod_step, p.value(KD, 4 * half + 4 - KD))
                        dst = aux[:, half * UNIT:(half + 1) * UNIT].rearrange("p (k n) -> p k n", k=4)
                        src = w[:, 4 * half:4 * half + 4, bass.ds(i.value(BANK), BANK)]
                        pool.dma_start(dst, src).then_inc(mod_landed[half], 16)

                piece(Count(p0), Count(0))
                with pool.Fori(0, N_PIECE // 2 - 1) as turn:
                    piece(Count(p0 + 1, 1, turn), Count(1, 1, turn))

            row(row_ffn, d["ffn1_post_norm"])
            modulation(0)
            pool.wait_ge(rel_zero, 1)
            pad = GRID - 1 - REL_C // 2
            for h in range(NA_H):
                pool.dma_start(rel[h * REL_USED:(h + 1) * REL_USED, pad:pad + REL_C],
                               d["na_rel_bias"][0, h, 8 - GRID_R:7 + GRID_R, :]).then_inc(rel_in, 16)
            pool.wait_ge(rel_in, 16 * NA_H)
            pool.dma_start(rel_dram.rearrange("r (q c) -> r q c", c=P),
                           rel.unsqueeze(1).broadcast_to([REL_USED * NA_H, GRID, P])).then_inc(rel_out, 16)
            pool.wait_ge(rel_out, 16)

            def bias_of(h):
                if h >= 2:
                    pool.wait_ge(at_m, h - 1)
                for r in range(GRID_R):
                    src = bass.AP(tensor=rel_dram.tensor, offset=(h * REL_USED + GRID_R - 1 - r) * GRID * P + GRID - 1,
                                  ap=[[P - 1, GRID], [GRID * P, GRID_R], [1, GRID]])
                    rows = slice((r % 2) * GRID, (r % 2 + 1) * GRID)
                    dst = bias[h % 2][rows, r // 2, :].rearrange("p (k c) -> p k c", c=GRID)
                    pool.dma_start(dst, src).then_inc(bias_in, 16)
                pool.wait_ge(bias_in, 64 * (h + 1))
                b = bias[h % 2].rearrange("p t (k c) -> p (t k) c", c=GRID)
                pool.tensor_tensor(b, b, na_mask[:, :].unsqueeze(1).broadcast_to([P, NT * 4, GRID]), ALU.add)\
                    .then_inc(bias_done, 1)

            pool.wait_ge(mod_step, KD * N_PIECE // 2)
            row(row_a, d["mix_post_norm"])
            for i in range(2):
                pool.dma_start(relu_t[i], d["relu_t"][i]).then_inc(ld_tab, 16)
            pool.dma_start(rot1.rearrange("p c t n -> p (c t n)"), d["rot1"]).then_inc(ld_tab, 16)
            for h in range(NA_H):
                bias_of(h)

            pool.wait_ge(norm_done[1], S_MIX + 1)
            row(row_ffn, d["ffn2_post_norm"])
            modulation(1)

            pool.wait_ge(norm_done[1], S_FFN2 + 1)
            pool.dma_start(causal, d["causal"]).then_inc(ld_tab, 16)
            pool.dma_start(rot2.rearrange("p c t n -> p (c t n)"), d["rot2"]).then_inc(ld_tab, 16)
            pool.wait_ge(mod_row, 1)
            pool.dma_start(mod_dram, mod_rows[:, :]).then_inc(mod_st, 16)
            pool.wait_ge(mod_st, 16)
            for n, s in enumerate((S_MOBA, S_MLP1, S_DIFF, S_MLP2)):
                layer, j = n // 2, n % 2
                r0 = 48 * layer + 24 * j + 16
                row(row_a, mod_dram[r0:r0 + KD, :].rearrange("k p -> (k p)").unsqueeze(0))
                row(row_g, d["ln_g_2"][layer, j:j + 1, :])
                row(row_b, d["ln_b_2"][layer, j:j + 1, :])
                if s == S_MLP2:
                    continue
                for t in range(NT):
                    pool.wait_ge(norm_done[t], s + 1)
                    pool.wait_ge(ld_row, 16 * 3 * (n + 2))
                    pool.tensor_tensor(x[:, t, :], zt[:, t, :], row_g, ALU.mult).then_inc(pool_step, 1)
                    pool.wait_ge(pool_step, NT * n + t + 1)
                    pool.tensor_tensor(x[:, t, :], x[:, t, :], row_b, ALU.add).then_inc(x_new, 1)
                pool.wait_ge(x_new, NT * (n + 1))


def _tables():
    tok = np.arange(SEQ)
    tables = {"ident": np.eye(P, dtype=np.float32)}
    qc = np.arange(P) % GRID
    start = np.clip(qc - 8, 0, GRID - 16)
    kc = np.arange(GRID)
    inside = (kc[None, :] >= start[:, None]) & (kc[None, :] < start[:, None] + 16)
    tables["na_mask"] = np.where(inside, 0.0, NEG).astype(np.float32)
    tri = np.where(np.arange(P)[None, :] <= np.arange(P)[:, None], 0.0, NEG).astype(np.float32)
    tables["causal"] = np.concatenate([tri, np.zeros_like(tri), tri], axis=1)
    dist = np.stack([tok[None, :] - (np.arange(P)[:, None] + P * m) for m in range(NT)], axis=1).reshape(P, NT * SEQ)
    tables["relu_t"] = np.stack([np.maximum(dist, 0), np.maximum(-dist, 0)]).astype(np.float32)

    def rotary(inv):
        ang = tok.astype(np.float32)[:, None] * inv[None, :]
        cs = np.stack([np.cos(ang), np.sin(ang)]).astype(np.float32)
        return cs.reshape(2, NT, P, -1).transpose(2, 0, 1, 3)

    lin = np.linspace(0.0, 1.0, RET_DK // 2, dtype=np.float32)
    tables["rot1"] = rotary((1.0 / (np.float32(10000.0) ** lin)).astype(np.float32)).reshape(P, -1)
    inv2 = np.float32(500000.0) ** (-np.arange(0, 2 * ROT, 2, dtype=np.float32) / np.float32(2 * ROT))
    r2 = rotary(inv2.astype(np.float32))
    tables["rot2"] = np.tile(r2[:, :, :, None, :], (1, 1, 1, 8, 1)).reshape(P, -1)
    return {k: np.ascontiguousarray(v) for k, v in tables.items()}


def kernel(**inputs):
    import concourse.bacc as bacc
    from concourse.bass_utils import run_bass_kernel_spmd as run

    nc = bacc.Bacc("TRN2", target_bir_lowering=False, num_devices=1)
    arrays, aps = {}, {}
    for name, value in {**inputs, **_tables()}.items():
        a = np.ascontiguousarray(value)
        arrays[f"in_{name}"] = a
        aps[name] = nc.dram_tensor(f"in_{name}", a.shape, mybir.dt.from_np(a.dtype), kind="ExternalInput").ap()
    out = nc.dram_tensor("out_0", (1, SEQ, D), F32, kind="ExternalOutput").ap()
    two_blocks_kernel(nc, aps, out)
    return run(nc, [arrays], core_ids=[0]).results[0]["out_0"]
```
